# Optimizing a Trainium2 kernel written in Bass

```python
import jax, jax.numpy as jnp
from jax import lax
import numpy as np

D_MODEL = 1024
BATCH = 1
SEQ = 256
DEPTH = 2

N_MIXERS = 2
N_CONV_LAYERS = (DEPTH + 1) // 2
N_POOL_LAYERS = DEPTH // 2
CONV_WIDTH = 3
POOL_WINDOWS = (2, 4, 8, 16)
N_POOL_GROUPS = len(POOL_WINDOWS)
POOL_GROUP_W = D_MODEL // N_POOL_GROUPS
N_KEYS = 128
N_EXPERTS = N_KEYS * N_KEYS
PEER_HEADS = 8
PEER_TOPK = 16
D_QUERY = 256
D_HALF = D_QUERY // 2
TOK_CHUNK = 128
N_MOD = 6
EPS = 1e-6

kernel_name = "hybrid_shortconv_pool_peer_adaln"

def rmsnorm(x, g):
    xf = x.astype(jnp.float32)
    y = xf * lax.rsqrt(jnp.mean(xf * xf, axis=-1, keepdims=True) + EPS)
    return (y * g.astype(jnp.float32)).astype(x.dtype)

def modulate(h, shift, scale):
    return h * (1.0 + scale[:, None, :]) + shift[:, None, :]

def short_conv_mixer(h, w_in, conv_w, w_out):
    S = h.shape[1]
    proj = h @ w_in
    b_gate, c_gate, u = jnp.split(proj, 3, axis=-1)
    v = c_gate * u
    vp = jnp.pad(v, ((0, 0), (CONV_WIDTH - 1, 0), (0, 0)))
    conv = conv_w[0] * vp[:, 0:S]
    for k in range(1, CONV_WIDTH):
        conv = conv + conv_w[k] * vp[:, k:k + S]
    return (b_gate * conv) @ w_out

def pool_mixer(h, w_in, w_grp, scale, w_out):
    B, S, D = h.shape
    u = (h @ w_in).reshape(B, S, N_POOL_GROUPS, POOL_GROUP_W)
    cs = jnp.cumsum(u.astype(jnp.float32), axis=1)
    t = jnp.arange(S)
    pooled = []
    for g, w in enumerate(POOL_WINDOWS):
        cg = cs[:, :, g]
        lag = jnp.pad(cg, ((0, 0), (w, 0), (0, 0)))[:, :S]
        cnt = jnp.minimum(t + 1, w).astype(jnp.float32)[None, :, None]
        pooled.append((cg - lag) / cnt)
    pooled = jnp.stack(pooled, axis=2).astype(u.dtype) - u
    z = jnp.einsum('bsgi,gio->bsgo', pooled, w_grp).reshape(B, S, D) * scale
    return z @ w_out

def peer_ffn(h, w_q, k1, k2, u_tab, v_tab):
    B, S, D = h.shape
    T = B * S
    ht = h.reshape(T, D)
    q = (ht @ w_q).reshape(T, PEER_HEADS, 2, D_HALF)
    s1 = jnp.einsum('thd,nd->thn', q[:, :, 0], k1)
    s2 = jnp.einsum('thd,nd->thn', q[:, :, 1], k2)
    v1, i1 = lax.top_k(s1, PEER_TOPK)
    v2, i2 = lax.top_k(s2, PEER_TOPK)
    cand = (v1[..., :, None] + v2[..., None, :]).reshape(T, PEER_HEADS, PEER_TOPK * PEER_TOPK)
    sc, flat = lax.top_k(cand, PEER_TOPK)
    e1 = jnp.take_along_axis(i1, flat // PEER_TOPK, axis=-1)
    e2 = jnp.take_along_axis(i2, flat % PEER_TOPK, axis=-1)
    idx = e1 * N_KEYS + e2
    gate = jax.nn.softmax(sc.astype(jnp.float32), axis=-1).astype(h.dtype)
    n_chunks = T // TOK_CHUNK

    def block(args):
        xc, ic, gc = args
        ug = u_tab[ic]
        act = jax.nn.gelu(jnp.einsum('td,thkd->thk', xc, ug), approximate=False)
        vg = v_tab[ic]
        return jnp.einsum('thk,thkd->td', gc * act, vg)

    out = lax.map(block, (ht.reshape(n_chunks, TOK_CHUNK, D),
                          idx.reshape(n_chunks, TOK_CHUNK, PEER_HEADS, PEER_TOPK),
                          gate.reshape(n_chunks, TOK_CHUNK, PEER_HEADS, PEER_TOPK)))
    return out.reshape(B, S, D)

def setup_inputs(seed: int = 0) -> dict:
    key = jax.random.key(seed)
    ks = jax.random.split(key, 20)
    D = D_MODEL
    nrm = lambda k, shape, s: jax.random.normal(k, shape, jnp.float32) * s
    inv = D ** -0.5
    return {
        "x": nrm(ks[0], (BATCH, SEQ, D), 1.0),
        "c": nrm(ks[1], (BATCH, D), 1.0),
        "norm1_g": 1.0 + nrm(ks[2], (DEPTH, D), 0.05),
        "norm2_g": 1.0 + nrm(ks[3], (DEPTH, D), 0.05),
        "w_mod": nrm(ks[4], (DEPTH, D, N_MOD * D), 0.5 * inv),
        "b_mod": nrm(ks[5], (DEPTH, N_MOD * D), 0.02),
        "conv_w_in": nrm(ks[6], (N_CONV_LAYERS, D, 3 * D), inv),
        "conv_w": nrm(ks[7], (N_CONV_LAYERS, CONV_WIDTH, D), CONV_WIDTH ** -0.5),
        "conv_w_out": nrm(ks[8], (N_CONV_LAYERS, D, D), inv),
        "pool_w_in": nrm(ks[9], (N_POOL_LAYERS, D, D), inv),
        "pool_w_grp": nrm(ks[10], (N_POOL_LAYERS, N_POOL_GROUPS, POOL_GROUP_W, POOL_GROUP_W), POOL_GROUP_W ** -0.5),
        "pool_scale": 1.0 + nrm(ks[11], (N_POOL_LAYERS, D), 0.1),
        "pool_w_out": nrm(ks[12], (N_POOL_LAYERS, D, D), inv),
        "peer_w_q": nrm(ks[13], (DEPTH, D, PEER_HEADS * D_QUERY), inv),
        "peer_k1": nrm(ks[14], (DEPTH, N_KEYS, D_HALF), D_HALF ** -0.5),
        "peer_k2": nrm(ks[15], (DEPTH, N_KEYS, D_HALF), D_HALF ** -0.5),
        "peer_u": nrm(ks[16], (DEPTH, N_EXPERTS, D), inv),
        "peer_v": nrm(ks[17], (DEPTH, N_EXPERTS, D), 0.5),
        "final_g": 1.0 + nrm(ks[18], (D,), 0.05),
    }

def reference(x, c, norm1_g, norm2_g, w_mod, b_mod, conv_w_in, conv_w, conv_w_out,
              pool_w_in, pool_w_grp, pool_scale, pool_w_out,
              peer_w_q, peer_k1, peer_k2, peer_u, peer_v, final_g):
    c_act = jax.nn.silu(c)
    for i in range(DEPTH):
        mod = c_act @ w_mod[i] + b_mod[i]
        sh1, sc1, g1, sh2, sc2, g2 = jnp.split(mod, N_MOD, axis=-1)
        h = modulate(rmsnorm(x, norm1_g[i]), sh1, sc1)
        j = i // N_MIXERS
        if i % N_MIXERS == 0:
            y = short_conv_mixer(h, conv_w_in[j], conv_w[j], conv_w_out[j])
        else:
            y = pool_mixer(h, pool_w_in[j], pool_w_grp[j], pool_scale[j], pool_w_out[j])
        x = x + g1[:, None, :] * y
        h = modulate(rmsnorm(x, norm2_g[i]), sh2, sc2)
        x = x + g2[:, None, :] * peer_ffn(h, peer_w_q[i], peer_k1[i], peer_k2[i], peer_u[i], peer_v[i])
    return rmsnorm(x, final_g)


_drawn_inputs = setup_inputs


def setup_inputs(seed=0):
    import zlib

    import numpy as np

    out = dict(_drawn_inputs(seed))
    spreads = {}
    factors = {}
    for name, (base, spread) in spreads.items():
        noise = np.random.default_rng([zlib.crc32(name.encode()), seed]).standard_normal(out[name].shape)
        drawn = base * np.exp(spread * noise) if base else spread * noise
        out[name] = __import__('jax').numpy.asarray(drawn.astype(out[name].dtype))
    for name, factor in factors.items():
        out[name] = (out[name] * factor).astype(out[name].dtype)
    return out
```

```python
from contextlib import ExitStack

import concourse.bass as bass
from concourse import mybir

F32 = mybir.dt.float32
F32R = mybir.dt.float32r
BF16 = mybir.dt.bfloat16
U32 = mybir.dt.uint32
ALU = mybir.AluOpType
ACT = mybir.ActivationFunctionType
AX_X = mybir.AxisListType.X

P = 128
D = 1024
DC = D // P
T = 256
TC = T // P
LAYERS = 2
MODS = 6
HEADS = 8
KEYS = 128
TOPK = 16
HALF = KEYS // 2
EPS = 1e-6
RING = 4
AHEAD = 3
WINDOWS = (2, 4, 8, 16)
PAD = max(WINDOWS)
TAPS = 3
SET = T // HALF
PARTS = 3
LOWEST = -3.0e38

C_C, C_N1, C_N2 = 0, 8, 24
C_BM = 40
C_CW = C_BM + LAYERS * MODS * DC
C_PS = C_CW + TAPS * DC
C_FG = C_PS + DC
C_IOTA = C_FG + DC
C_EYE = C_IOTA + P
C_CNT = C_EYE + P
SMALL = C_CNT + len(WINDOWS) * PAD

STREAM = [[("conv_in", 24), ("conv_out", 8), ("query", 16), ("up", KEYS), ("down", KEYS)],
          [("pool_in", 8), ("pool_group", 4), ("pool_out", 8), ("query", 16), ("up", KEYS), ("down", KEYS)]]


def places():
    at, n = {}, 0
    for layer, runs in enumerate(STREAM):
        for name, tiles in runs:
            at[layer, name] = n
            n += tiles
    return at, n


class Chain:

    def __init__(self, eng, sem):
        self.eng, self.sem, self.base, self.k, self.i, self.per = eng, sem, 0, 0, None, 0

    def value(self):
        return self.base + self.k if self.i is None else self.i * self.per + (self.base + self.k)

    def __call__(self, ins, met=None):
        self.k += 1
        ins.then_inc(self.sem, 1)
        value = self.value()
        if met is not None:
            self.eng.compute_val(value)
            self.eng.wait_ge(*met)
        self.eng.wait_ge(self.sem, value)

    def enter(self, i, per):
        self.base, self.k, self.i, self.per = self.base + self.k, 0, i, per

    def leave(self, trips):
        assert self.k == self.per, (self.k, self.per)
        self.base, self.k, self.i = self.base + self.per * trips, 0, None


def program(nc, small, x_in, k_t, w_mod, conv_in, conv_out, query, up, down, pool_in, pool_group, pool_out,
            x_spill, out):
    AT, TILES = places()
    tiles_of = {("conv_in", 0): conv_in, ("conv_out", 0): conv_out, ("pool_in", 1): pool_in,
                ("pool_group", 1): pool_group, ("pool_out", 1): pool_out}
    for layer in range(LAYERS):
        for name, src in (("query", query), ("up", up), ("down", down)):
            tiles_of[name, layer] = src[layer]

    with ExitStack() as ctx:
        def sb(name, shape, dt):
            return ctx.enter_context(nc.sbuf_tensor(name, shape, dt))

        def sem(name):
            return ctx.enter_context(nc.semaphore(name))

        A = sb("acts", [P, KEYS * T], F32)
        raw = sb("raw", [P, RING, D], F32)
        high = [sb(f"high{s}", [P, DC, P], F32R) for s in range(RING)]
        low = [sb(f"low{s}", [P, DC, P], F32R) for s in range(RING)]
        mov_h = sb("mov_h", [P, DC, T], F32R)
        mov_l = sb("mov_l", [P, DC, T], F32R)
        sm = sb("sm", [P, SMALL], F32)
        keys = sb("keys", [P, 2, P], F32)
        mod = sb("mod", [P, MODS * DC], F32)
        gs = sb("gs", [P, DC], F32)
        cact = sb("cact", [P, DC], F32)
        ctmp = sb("ctmp", [P, DC], F32)
        eps = sb("eps", [P, 1], F32)
        ones = sb("ones", [P, P], F32)
        zeros = sb("zeros", [P, P], BF16)
        idx1 = sb("idx1", [P, T], BF16)
        idx2 = sb("idx2", [P, T], BF16)
        gate = sb("gate", [P, PARTS, T], BF16)
        gate_rest = sb("gate_rest", [P, T], F32)
        eq1 = sb("eq1", [P, 2, SET, HALF], BF16)
        hot1 = sb("hot1", [P, 2, PARTS, SET, HALF], BF16)
        hot2 = sb("hot2", [P, 2, SET, P], BF16)

        iota = sm[:, C_IOTA:C_IOTA + P]
        eye = sm[:, C_EYE:C_EYE + P]

        def part(a, n):
            return A[:, a:a + n]

        X = part(0, DC * T).rearrange("p (c t) -> p c t", c=DC)
        mtile = part(2048, 2 * D).rearrange("p (s n) -> p s n", s=2)
        ntile = part(10240, MODS * D).rearrange("p (s n) -> p s n", s=MODS)
        macc = part(4096, MODS * D).rearrange("p (m n) -> p m n", m=MODS)
        B0 = HALF * T
        mhead = part(B0, 2 * DC * D).rearrange("p (m k n) -> p m k n", m=2, k=DC)
        xr = part(13312, DC * T).rearrange("p (c t) -> p c t", c=DC)
        sq = part(11264, DC * T).rearrange("p (c t) -> p c t", c=DC)
        sd = part(10240, TC)
        rstd = part(10240 + TC, TC)
        diag = part(10240 + 2 * TC, T).rearrange("p (c t) -> p c t", c=TC)
        vp = part(B0, 2 * (T + 2)).rearrange("p (s t) -> p s t", s=2)
        cs = part(B0 + 1024, 2 * T).rearrange("p (s t) -> p s t", s=2)
        cv = part(B0 + 1536, 3 * T).rearrange("p (s t) -> p s t", s=3)
        Z = part(B0 + 2560, DC * T).rearrange("p (c t) -> p c t", c=DC)
        UP = part(B0 + 4864, DC * (PAD + T)).rearrange("p (c t) -> p c t", c=DC)
        W1 = part(B0 + 7168, 2 * (PAD + T)).rearrange("p (c t) -> p c t", c=2)
        W2 = part(B0 + 7936, 2 * (PAD + T)).rearrange("p (c t) -> p c t", c=2)
        WS = part(B0 + 8704, 2 * PAD).rearrange("p (c t) -> p c t", c=2)
        ROWS = TC * HEADS
        S = part(B0, ROWS * 2 * KEYS)
        Q = part(B0 + 8192, 2 * HEADS * T).rearrange("p (n t) -> p n t", n=2 * HEADS)
        EQ = part(B0 + 8192, T * TOPK)
        o = B0 + 12288
        SC = part(o, T)
        FL = part(o + 256, T).bitcast(U32)
        IDX = part(o + 512, 2 * T)
        ABu = part(o + 1024, 2 * T).bitcast(U32)
        AB = part(o + 1536, 2 * T)
        EX = part(o + 2048, 2 * T)
        GT = part(o + 2560, T)
        SUM = part(o + 2816, ROWS)
        RS = part(o + 2832, ROWS)
        s2 = part(o + 2848, 2 * KEYS).rearrange("p (s n) -> p s n", s=2)
        s3 = part(o + 3104, 2 * KEYS).rearrange("p (s n) -> p s n", s=2)
        v16 = part(o + 3360, 2 * TOPK).rearrange("p (s n) -> p s n", s=2)
        i16 = part(o + 3392, 2 * TOPK).rearrange("p (s n) -> p s n", s=2).bitcast(U32)
        cand = part(o + 3424, TOPK * TOPK)
        cand2 = part(o + 3680, TOPK * TOPK)
        b16 = part(o + 3936, TOPK)
        f16 = part(o + 3952, TOPK).bitcast(U32)

        def psum(name, n):
            return ctx.enter_context(nc.psum_tensor(name, [P, n, 512], F32))

        ps = psum("ps", 2)
        gp = psum("gp", 2)
        acc = psum("acc", 4)

        raw_full = [sem(f"raw_full{s}") for s in range(RING)]
        high_ready = sem("high_ready")
        low_ready = sem("low_ready")
        product = sem("product")
        evac_dve = sem("evac_dve")
        evac_act = sem("evac_act")
        small_in, x_in_s, keys_in = sem("small_in"), sem("x_in_s"), sem("keys_in")
        mhead_in = [sem(f"mhead_in{n}") for n in range(4)]
        mtile_in = [sem(f"mtile_in{n}") for n in range(2)]
        mtile_used = sem("mtile_used")
        next_in = [sem(f"next_in{n}") for n in range(MODS)]
        next_used = sem("next_used")
        macc_done, msum_done = sem("macc_done"), sem("msum_done")
        const_ready = sem("const_ready")
        cexp = sem("cexp")
        x_ready = sem("x_ready")
        sq_done, stat_done, sd_done = sem("sq_done"), sem("stat_done"), sem("sd_done")
        xr_done, mh_done, ml_done = sem("xr_done"), sem("mh_done"), sem("ml_done")
        z_ready = sem("z_ready")
        score_done, score_out = sem("score_done"), sem("score_out")
        soft_in, soft_exp = sem("soft_in"), sem("soft_exp")
        pick_done, turned, turned_out = sem("pick_done"), sem("turned"), sem("turned_out")
        hot1_ready = sem("hot1_ready")
        hot_eq = sem("hot_eq")
        scattered, weighted = sem("scattered"), sem("weighted")
        wh_ready, wl_ready = sem("wh_ready"), sem("wl_ready")
        spilled, reloaded = sem("spilled"), sem("reloaded")
        acc_done = sem("acc_done")
        step = sem("step")
        diag_done, rs_done = sem("diag_done"), sem("rs_done")
        stored = sem("stored")

        def tile_row(s):
            return raw[:, s]

        def flat(t):
            return t[:].rearrange("p a b -> p (a b)")

        block = ctx.enter_context(nc.Block())

        @block.sync
        def _(sp):
            sp.sem_inc(mtile_used, 2)
            sp.sem_inc(next_used, MODS)
            sp.dma_start(sm[:], small).then_inc(small_in, 16)
            sp.dma_start(A[:, 0:DC * T], x_in).then_inc(x_in_s, 16)
            for n, (m, k) in enumerate(((0, 0), (0, 4), (1, 0), (1, 4))):
                sp.dma_start(mhead[:, m, k:k + 4],
                             w_mod[0, k * P:(k + 4) * P, m * D:(m + 1) * D].rearrange("(k p) n -> p k n", p=P)
                             ).then_inc(mhead_in[n], 16)

            def load(layer, name, j, s):
                n0 = AT[layer, name]
                static = isinstance(j, int)
                if not (static and n0 + j < RING):
                    sp.wait_ge(low_ready, j + (n0 - RING + 1))
                src = tiles_of[name, layer]
                src = src[j] if static else src[bass.ds(j, 1)].rearrange("a p n -> (a p) n")
                sp.dma_start(tile_row(s), src).then_inc(raw_full[s], 16)

            def load_mod(layer, m, k, t, slot):
                sp.wait_ge(mtile_used, t + 1)
                sp.dma_start(mtile[:, slot], w_mod[layer, k * P:(k + 1) * P, m * D:(m + 1) * D]
                             ).then_inc(mtile_in[slot], 16)

            late = 3
            for t in range(32 + late):
                if t < 24:
                    load(0, "conv_in", t, t % RING)
                elif t < 32:
                    load(0, "conv_out", t - 24, t % RING)
                if t >= late:
                    u = t - late
                    load_mod(0, 2 + u % 3 if u < 24 else 5, u // 3 if u < 24 else u - 24, u, u % 2)

            def run(layer, name, tiles, first=0):
                with sp.Fori(0, tiles // RING) as i:
                    for s in range(RING):
                        load(layer, name, i * RING + (first + s), s)

            for layer in range(LAYERS):
                if layer == 1:
                    run(1, "pool_in", 8)
                    run(1, "pool_group", 4)
                    run(1, "pool_out", 8)
                run(layer, "query", 16)
                run(layer, "up", KEYS)
                if layer == 1:
                    run(1, "down", KEYS)
                else:
                    run(0, "down", HALF)
                    sp.wait_ge(wl_ready, HALF)
                    with sp.Fori(0, DC) as i:
                        for q in range(8):
                            load(0, "down", i * 8 + (HALF + q), q % RING)
                            if q < MODS:
                                sp.wait_ge(next_used, i * MODS + (q + 1))
                                w = w_mod[1, :, q * D:(q + 1) * D].rearrange("(k p) n -> k p n", p=P)
                                sp.dma_start(ntile[:, q], w[bass.ds(i, 1)].rearrange("a p n -> (a p) n")
                                             ).then_inc(next_in[q], 16)
            for n in range(4):
                sp.wait_ge(xr_done, 4 * DC + 2 * n + 2)
                sp.dma_start(out[:, 2 * n * T:(2 * n + 2) * T],
                             A[:, B0 + 2 * n * T:B0 + (2 * n + 2) * T]).then_inc(stored, 16)
            sp.wait_ge(stored, 4 * 16)

        @block.gpsimd
        def _(pool):
            nc.gpsimd.memset(ones[:], 1.0).then_inc(const_ready, 1)
            nc.gpsimd.memset(eps[:], EPS).then_inc(const_ready, 1)
            nc.gpsimd.memset(zeros[:], 0.0).then_inc(const_ready, 1)
            nc.gpsimd.memset(macc[:, 2:MODS].rearrange("p m n -> p (m n)"), 0.0).then_inc(const_ready, 1)
            with pool.Fori(0, TILES // RING) as i:
                for s in range(RING):
                    pool.wait_ge(high_ready, i * RING + (s + 1))
                    nc.gpsimd.tensor_tensor(flat(low[s]), tile_row(s), flat(high[s]).bitcast(F32),
                                            ALU.subtract).then_inc(low_ready, 1)

        @block.scalar
        def _(act):
            act.sem_inc(evac_act, 2)
            act.sem_inc(evac_dve, 2)

            def round_tile(n, s):
                act.wait_ge(product, n + 1)
                nc.scalar.activation(flat(high[s]), tile_row(s), ACT.Copy).then_inc(high_ready, 1)

            def arrived(k, s):
                act.wait_ge(raw_full[s], k * 16)

            def ahead(i, n0, s):
                t = s + AHEAD
                arrived(i + (n0 // RING + t // RING + 1), t % RING)
                round_tile(i * RING + (n0 + t), t % RING)

            def norm(k):
                for c in range(DC):
                    if k == 0:
                        act.wait_ge(x_in_s, 16)
                    elif k % 2:
                        act.wait_ge(evac_dve, 2 + (24 if k == 1 else 44) + c + 1)
                    else:
                        act.wait_ge(x_ready, (k // 2 - 1) * DC + c + 1)
                    nc.scalar.activation(sq[:, c], X[:, c], ACT.Square).then_inc(sq_done, 1)
                if k in (1, 3):
                    act.dma_start(x_spill, flat2(X)).then_inc(spilled, 16)
                act.wait_ge(stat_done, k + 1)
                nc.scalar.activation(sd, gp[:, 0, 0:TC], ACT.Sqrt, bias=eps[:, 0:1],
                                     scale=1.0 / D).then_inc(sd_done, 1)
                if k == 4:
                    return
                shift = mod[:, (3 * (k % 2)) * DC:(3 * (k % 2) + 1) * DC]
                for c in range(DC):
                    act.wait_ge(xr_done, DC * k + c + 1)
                    nc.scalar.activation(mov_h[:, c], xr[:, c], ACT.Identity,
                                         bias=shift[:, c:c + 1]).then_inc(mh_done, 1)

            def flat2(v):
                return v.rearrange("p c t -> p (c t)")

            def split_z(n_products, ready):
                act.wait_ge(product, n_products + RING)
                for c in range(DC):
                    act.wait_ge(*ready(c))
                    nc.scalar.activation(mov_h[:, c], Z[:, c], ACT.Copy).then_inc(mh_done, 1)

            def only_round(n0, tiles):
                with act.Fori(0, tiles // RING) as i:
                    for s in range(RING):
                        ahead(i, n0, s)

            act.dma_start(keys[:], k_t[0]).then_inc(keys_in, 16)
            act.wait_ge(small_in, 16)
            nc.scalar.activation(ctmp[:], sm[:, C_C:C_C + DC], ACT.Exp, scale=-1.0).then_inc(cexp, 1)
            for n in range(AHEAD):
                arrived(1, n)
                nc.scalar.activation(flat(high[n]), tile_row(n), ACT.Copy).then_inc(high_ready, 1)
            for layer in range(LAYERS):
                norm_k = 2 * layer
                if layer == 0:
                    act.wait_ge(const_ready, 4)
                norm(norm_k)
                if layer == 0:
                    only_round(AT[0, "conv_in"], 24)
                    split_z(AT[0, "conv_out"], lambda c: (evac_dve, 2 + 3 * (c + 1)))
                    only_round(AT[0, "conv_out"], 8)
                else:
                    only_round(AT[1, "pool_in"], 8)
                    split_z(AT[1, "pool_group"], lambda c: (z_ready, c + 1))
                    only_round(AT[1, "pool_group"], 4)
                    split_z(AT[1, "pool_out"], lambda c: (evac_dve, 2 + 32 + 8 + c // 2 + 1))
                    only_round(AT[1, "pool_out"], 8)
                norm(norm_k + 1)
                n0 = AT[layer, "query"]
                with act.Fori(0, 16 // RING) as i:
                    for s in range(RING):
                        ahead(i, n0, s)
                        act.wait_ge(product, i * RING + (n0 + s + 1 + RING))
                        nc.scalar.activation(A[:, bass.ds(i * (RING * T) + (B0 + 8192 + s * T), T)],
                                             ps[:, s % 2, 0:T], ACT.Copy).then_inc(evac_act, 1)
                act.wait_ge(spilled, 16 * (layer + 1))
                n0 = AT[layer, "up"]

                def gelus(first, trips):
                    with act.Fori(0, trips) as i:
                        for s in range(RING):
                            ahead(i, n0 + first, s)
                            act.wait_ge(product, i * RING + (n0 + first + s + 1 + RING))
                            nc.scalar.activation(A[:, bass.ds(i * (RING * T) + (first + s) * T, T)],
                                                 ps[:, s % 2, 0:T], ACT.Gelu).then_inc(evac_act, 1)

                gelus(0, HALF // RING - 4)
                act.wait_ge(soft_in, layer + 1)
                nc.scalar.activation(SC, SC, ACT.Exp).then_inc(soft_exp, 1)
                gelus(HALF - 4 * RING, 4)
                act.wait_ge(turned, layer + 1)
                if layer == 0:
                    act.dma_start(keys[:], k_t[1]).then_inc(keys_in, 16)
                gelus(HALF, HALF // RING)

                n0 = AT[layer, "down"]

                def weight(g, s):
                    nc.scalar.activation(mov_h[:, s], A[:, bass.ds(g * T, T)] if not isinstance(g, int)
                                         else A[:, g * T:(g + 1) * T], ACT.Copy).then_inc(wh_ready, 1)

                for half in range(2):
                    first = half * HALF
                    act.wait_ge(weighted, (2 * layer + half + 1) * HALF)
                    for s in range(AHEAD):
                        act.wait_ge(product, n0 + first + s + 1 + (RING - 1 - s if half == 0 else 0))
                        weight(first + s, s)
                    with act.Fori(0, HALF // RING - 1) as i:
                        for s in range(RING):
                            ahead(i, n0 + first, s)
                            weight(i * RING + (first + s + AHEAD), (s + AHEAD) % RING)
                    last = n0 + first + HALF - RING
                    for s in range(RING):
                        if last + s + AHEAD < TILES:
                            ahead(0, last, s)
                        if s + AHEAD < RING:
                            if last + s + AHEAD >= TILES:
                                act.wait_ge(product, last + s + AHEAD + 1)
                            weight(first + HALF - RING + s + AHEAD, (s + AHEAD) % RING)
                    if half == 0:
                        act.wait_ge(wl_ready, (2 * layer + 1) * HALF)
                        act.dma_start(A[:, 0:DC * T], x_spill).then_inc(reloaded, 16)
            norm(4)

        @block.vector
        def _(dve):
            link = Chain(dve, step)

            def turn(v, n):
                return v.rearrange("p (r n) -> p r n", n=n)

            dve.wait_ge(cexp, 1)
            link(nc.vector.tensor_scalar(ctmp[:], ctmp[:], 1.0, None, ALU.add))
            link(nc.vector.reciprocal(ctmp[:], ctmp[:]))
            link(nc.vector.tensor_tensor(cact[:], ctmp[:], sm[:, C_C:C_C + DC], ALU.mult))

            def add_mod(m, tile, k, first):
                c = cact[:, k:k + 1] if isinstance(k, int) else cact[:, bass.ds(k, 1)]
                if first:
                    return nc.vector.tensor_scalar(macc[:, m], tile, c, None, ALU.mult)
                return nc.vector.scalar_tensor_tensor(macc[:, m], tile, c, macc[:, m], ALU.mult, ALU.add)

            for m in range(2):
                for k in range(DC):
                    if k % 4 == 0:
                        dve.wait_ge(mhead_in[2 * m + k // 4], 16)
                    link(add_mod(m, mhead[:, m, k], k, k == 0))
                dve.sem_inc(macc_done, 1)

            sums = [0]

            def finish_mod(layer, ms):
                sums[0] += 1
                dve.wait_ge(msum_done, sums[0])
                a, b = ms[0] * DC, (ms[-1] + 1) * DC
                bm = C_BM + layer * MODS * DC
                link(nc.vector.tensor_tensor(mod[:, a:b], gp[:, 1, a:b], sm[:, bm + a:bm + b], ALU.add))

            def norm(k):
                g0 = (C_N1, C_N2)[k % 2] + (k // 2) * DC
                if k < 4:
                    scale = mod[:, (3 * (k % 2) + 1) * DC:(3 * (k % 2) + 2) * DC]
                    link(nc.vector.scalar_tensor_tensor(gs[:], scale, 1.0, sm[:, g0:g0 + DC], ALU.add, ALU.mult))
                    weight = gs[:]
                else:
                    weight = sm[:, C_FG:C_FG + DC]
                dve.wait_ge(sd_done, k + 1)
                link(nc.vector.reciprocal(rstd, sd))
                for tc in range(TC):
                    nc.vector.tensor_scalar(diag[:, tc], eye, rstd[:, tc:tc + 1], None, ALU.mult
                                            ).then_inc(diag_done, 1)
                dve.wait_ge(rs_done, k + 1)
                if k < 4:
                    shift = mod[:, (3 * (k % 2)) * DC:(3 * (k % 2) + 1) * DC]

                def scaled(c):
                    dst = xr[:, c] if k < 4 else A[:, B0 + c * T:B0 + (c + 1) * T]
                    nc.vector.scalar_tensor_tensor(dst, X[:, c], weight[:, c:c + 1], gp[:, 0, T:2 * T], ALU.mult,
                                                   ALU.mult).then_inc(xr_done, 1)

                def rest(c):
                    moved[0] += 1
                    dve.wait_ge(mh_done, moved[0])
                    nc.vector.scalar_tensor_tensor(mov_l[:, c], xr[:, c], shift[:, c:c + 1],
                                                   mov_h[:, c].bitcast(F32), ALU.add,
                                                   ALU.subtract).then_inc(ml_done, 1)

                for c in range(DC):
                    scaled(c)
                    if k < 4 and c >= 2:
                        rest(c - 2)
                if k < 4:
                    rest(DC - 2)
                    rest(DC - 1)

            moved = [0]

            def split_z():
                for c in range(DC):
                    moved[0] += 1
                    dve.wait_ge(mh_done, moved[0])
                    nc.vector.tensor_tensor(mov_l[:, c], Z[:, c], mov_h[:, c].bitcast(F32),
                                            ALU.subtract).then_inc(ml_done, 1)

            def bank(n0, j, s):
                dve.wait_ge(product, j + (n0 + 1 + RING))
                return ps[:, s % 2, 0:T]

            def use_mtile(m, k, t, slot):
                dve.wait_ge(mtile_in[slot], t)
                add_mod(m, mtile[:, slot], k, False).then_inc(mtile_used, 1)

            def residual(n0, m, trips):
                with dve.Fori(0, trips) as i:
                    for s in range(RING):
                        p = bank(n0, i * RING + s, s)
                        x = A[:, bass.ds(i * (RING * T) + s * T, T)]
                        g = mod[:, bass.ds(i * RING + (m * DC + s), 1)]
                        nc.vector.scalar_tensor_tensor(x, p, g, x, ALU.mult, ALU.add).then_inc(evac_dve, 1)

            def picks(rows):
                met = (score_out, 1)
                for src, spare, vals, idx in rows:
                    ins = nc.vector.max(vals[:, 0:8], src)
                link(ins, met=met)
                for src, spare, vals, idx in rows:
                    nc.vector.max_index(idx[:, 0:8], vals[:, 0:8], src)
                    ins = nc.vector.match_replace(spare, vals[:, 0:8], src, LOWEST)
                link(ins, met=met)
                for src, spare, vals, idx in rows:
                    ins = nc.vector.max(vals[:, 8:16], spare)
                link(ins, met=met)
                for src, spare, vals, idx in rows:
                    ins = nc.vector.max_index(idx[:, 8:16], vals[:, 8:16], spare)
                return ins

            for layer in range(LAYERS):
                if layer == 0:
                    finish_mod(0, (0, 1))
                    norm(0)
                    n0 = AT[0, "conv_in"]
                    link(nc.vector.memset(vp, 0.0))
                    with dve.Fori(0, 2) as i:
                        link.enter(i, 12)
                        for q in range(4):
                            s = 3 * q
                            w = [sm[:, bass.ds(i * 4 + (C_CW + k * DC + q), 1)] for k in range(TAPS)]
                            z = A[:, bass.ds(i * (4 * T) + (B0 + 2560 + q * T), T)]
                            p = bank(n0, i * 12 + s, s)
                            nc.vector.tensor_copy(cs[:, q % 2], p).then_inc(evac_dve, 1)
                            use_mtile(2, i * 4 + q, i * (6 * 16) + (s // 2 + 1) * 16, s % 2)
                            p = bank(n0, i * 12 + s + 1, s + 1)
                            dve.wait_ge(evac_dve, i * 12 + (2 + s + 1))
                            nc.vector.tensor_tensor(vp[:, q % 2, 2:2 + T], p, cs[:, q % 2],
                                                    ALU.mult).then_inc(evac_dve, 1)
                            use_mtile(3, i * 4 + q, i * (6 * 16) + ((s + 1) // 2 + 1) * 16, (s + 1) % 2)
                            dve.wait_ge(evac_dve, i * 12 + (2 + s + 2))
                            link(nc.vector.tensor_scalar(cv[:, 0], vp[:, q % 2, 0:T], w[0], None, ALU.mult))
                            link(nc.vector.scalar_tensor_tensor(cv[:, 1], vp[:, q % 2, 1:1 + T], w[1], cv[:, 0],
                                                                ALU.mult, ALU.add))
                            link(nc.vector.scalar_tensor_tensor(cv[:, 2], vp[:, q % 2, 2:2 + T], w[2], cv[:, 1],
                                                                ALU.mult, ALU.add))
                            p = bank(n0, i * 12 + s + 2, s + 2)
                            nc.vector.tensor_tensor(z, p, cv[:, 2], ALU.mult).then_inc(evac_dve, 1)
                            use_mtile(4, i * 4 + q, i * (6 * 16) + ((s + 2) // 2 + 1) * 16, (s + 2) % 2)
                            dve.wait_ge(mtile_used, i * 12 + (2 + s + 3))
                        link.leave(2)
                    split_z()
                    finish_mod(0, (2, 3, 4))
                    n0 = AT[0, "conv_out"]
                    with dve.Fori(0, 2) as i:
                        for s in range(RING):
                            p = bank(n0, i * RING + s, s)
                            x = A[:, bass.ds(i * (RING * T) + s * T, T)]
                            g = mod[:, bass.ds(i * RING + (2 * DC + s), 1)]
                            nc.vector.scalar_tensor_tensor(x, p, g, x, ALU.mult, ALU.add).then_inc(evac_dve, 1)
                            use_mtile(5, i * RING + s, i * (2 * 16) + (s // 2 + 13) * 16, s % 2)
                            dve.wait_ge(mtile_used, i * RING + (2 + 24 + s + 1))
                    finish_mod(0, (5,))
                else:
                    dve.wait_ge(x_ready, DC)
                    finish_mod(1, tuple(range(MODS)))
                    norm(2)
                    n0 = AT[1, "pool_in"]
                    link(nc.vector.memset(UP[:, :, 0:PAD], 0.0))
                    for g, w in enumerate(WINDOWS):
                        for j in (2 * g, 2 * g + 1):
                            p = bank(n0, j, j)
                            nc.vector.tensor_copy(UP[:, j, PAD:PAD + T], p).then_inc(evac_dve, 1)
                        dve.wait_ge(evac_dve, 2 + 32 + 2 * g + 2)
                        src, span, spare = UP[:, 2 * g:2 * g + 2], 1, [W1, W2]
                        end = PAD + T
                        while span < w:
                            dst = spare[0]
                            lo = 2 * span - 1
                            link(nc.vector.tensor_tensor(dst[:, :, lo:end], src[:, :, lo:end],
                                                         src[:, :, lo - span:end - span], ALU.add))
                            src, span, spare = dst, 2 * span, spare[::-1]
                        u = UP[:, 2 * g:2 * g + 2]
                        z = Z[:, 2 * g:2 * g + 2]
                        counts = sm[:, C_CNT + g * PAD:C_CNT + (g + 1) * PAD].unsqueeze(1).broadcast_to([P, 2, PAD])
                        link(nc.vector.tensor_tensor(WS, src[:, :, PAD:2 * PAD], counts, ALU.mult))
                        link(nc.vector.scalar_tensor_tensor(z, src[:, :, PAD:end], 1.0 / w, u[:, :, PAD:end],
                                                            ALU.mult, ALU.subtract))
                        nc.vector.tensor_tensor(z[:, :, 0:PAD], WS, u[:, :, PAD:2 * PAD],
                                                ALU.subtract).then_inc(z_ready, 2)
                    split_z()
                    n0 = AT[1, "pool_group"]
                    for j in range(4):
                        dve.wait_ge(product, n0 + j + 1 + RING)
                        for c in range(2):
                            ins = nc.vector.tensor_scalar(Z[:, 2 * j + c], ps[:, j % 2, c * T:(c + 1) * T],
                                                          sm[:, C_PS + 2 * j + c:C_PS + 2 * j + c + 1], None, ALU.mult)
                        ins.then_inc(evac_dve, 1)
                    split_z()
                    residual(AT[1, "pool_out"], 2, 2)
                norm(2 * layer + 1)

                for n in range(8):
                    dve.wait_ge(score_done, 8 * layer + n + 1)
                    nc.vector.tensor_copy(S[:, n * 512:(n + 1) * 512], gp[:, n % 2, :]).then_inc(score_out, 1)
                dve.wait_ge(score_out, 8 * (layer + 1))
                with dve.Fori(0, ROWS) as i:
                    link.enter(i, 10)
                    link(nc.vector.tensor_copy(s2.rearrange("p s n -> p (s n)"),
                                               A[:, bass.ds(i * (2 * KEYS) + B0, 2 * KEYS)]), met=(score_out, 1))
                    picks([(s2[:, side], s3[:, side], v16[:, side], i16[:, side]) for side in range(2)])
                    link(nc.vector.tensor_tensor(cand.rearrange("p (a b) -> p a b", a=TOPK),
                                                 v16[:, 0].unsqueeze(2).broadcast_to([P, TOPK, TOPK]),
                                                 v16[:, 1].unsqueeze(1).broadcast_to([P, TOPK, TOPK]), ALU.add),
                         met=(score_out, 1))
                    link(picks([(cand, cand2, b16, f16)]))
                    nc.vector.tensor_copy(A[:, bass.ds(i * TOPK + o, TOPK)], b16)
                    nc.vector.tensor_copy(A[:, bass.ds(i * TOPK + (o + 256), TOPK)].bitcast(U32), f16)
                    link(nc.vector.tensor_copy(A[:, bass.ds(i * (2 * TOPK) + (o + 512), 2 * TOPK)],
                                               i16.rearrange("p s n -> p (s n)")))
                    link.leave(ROWS)
                sc3 = turn(SC, TOPK)
                link(nc.vector.tensor_copy(RS, sc3[:, :, 0]))
                nc.vector.tensor_tensor(sc3, sc3, RS.unsqueeze(2).broadcast_to([P, ROWS, TOPK]),
                                        ALU.subtract).then_inc(soft_in, 1)
                nc.vector.tensor_scalar(ABu[:, 0:T], FL, 4, None, ALU.logical_shift_right)
                link(nc.vector.tensor_scalar(ABu[:, T:2 * T], FL, TOPK - 1, None, ALU.bitwise_and))
                link(nc.vector.tensor_copy(AB, ABu))
                idx4 = IDX.rearrange("p (r s n) -> p r s n", s=2, n=TOPK)
                for side in range(2):
                    eq = EQ.rearrange("p (r k) -> p r k", k=TOPK)
                    link(nc.vector.tensor_tensor(eq, AB[:, side * T:(side + 1) * T].unsqueeze(2)
                                                 .broadcast_to([P, T, TOPK]),
                                                 iota[:, 0:TOPK].unsqueeze(1).broadcast_to([P, T, TOPK]),
                                                 ALU.is_equal))
                    eq4 = EQ.rearrange("p (r k n) -> p r k n", k=TOPK, n=TOPK)
                    link(nc.vector.tensor_tensor(eq4, eq4, idx4[:, :, side].unsqueeze(2)
                                                 .broadcast_to([P, ROWS, TOPK, TOPK]), ALU.mult))
                    link(nc.vector.tensor_reduce(EX[:, side * T:(side + 1) * T], eq, AX_X, ALU.add))
                dve.wait_ge(soft_exp, layer + 1)
                link(nc.vector.tensor_reduce(SUM, sc3, AX_X, ALU.add))
                link(nc.vector.reciprocal(RS, SUM))
                nc.vector.tensor_tensor(turn(GT, TOPK), sc3, RS.unsqueeze(2).broadcast_to([P, ROWS, TOPK]),
                                        ALU.mult).then_inc(pick_done, 1)
                dve.wait_ge(turned, layer + 1)
                nc.vector.tensor_copy(idx1[:], gp[:, 0, 0:T]).then_inc(turned_out, 1)
                nc.vector.tensor_copy(idx2[:], gp[:, 0, T:2 * T]).then_inc(turned_out, 1)
                link(nc.vector.tensor_copy(gate[:, 0], gp[:, 1, 0:T]))
                nc.vector.tensor_tensor(gate_rest[:], gp[:, 1, 0:T], gate[:, 0], ALU.subtract).then_inc(turned_out, 1)
                dve.wait_ge(turned_out, 3 * (layer + 1))
                link(nc.vector.tensor_copy(gate[:, 1], gate_rest[:]))
                link(nc.vector.tensor_tensor(gate_rest[:], gate_rest[:], gate[:, 1], ALU.subtract))
                link(nc.vector.tensor_copy(gate[:, 2], gate_rest[:]))

                def hots(half, i, s):
                    def over(v, n):
                        v = v[:, bass.ds(i * (RING * SET) + s * SET, SET)]
                        return v.unsqueeze(2).broadcast_to([P, SET, n])

                    def number(a, b):
                        return iota[:, a:b].unsqueeze(1).broadcast_to([P, SET, b - a])

                    k0 = (2 * layer + half) * HALF
                    nc.vector.tensor_tensor(eq1[:, s % 2], number(half * HALF, (half + 1) * HALF), over(idx1, HALF),
                                            ALU.is_equal).then_inc(hot_eq, 1)
                    nc.vector.tensor_tensor(hot2[:, s % 2], number(0, P), over(idx2, P), ALU.is_equal)
                    dve.wait_ge(hot_eq, i * RING + (k0 + s + 1))
                    g = gate[:, :, bass.ds(i * (RING * SET) + s * SET, SET)]
                    nc.vector.tensor_tensor(hot1[:, s % 2],
                                            eq1[:, s % 2].unsqueeze(1).broadcast_to([P, PARTS, SET, HALF]),
                                            g.unsqueeze(3).broadcast_to([P, PARTS, SET, HALF]), ALU.mult
                                            ).then_inc(hot1_ready, 1)

                def weigh(half, i, s):
                    k0 = (2 * layer + half) * HALF
                    dve.wait_ge(scattered, i * RING + (k0 + s + 1))
                    a = A[:, half * B0:half * B0 + HALF * T].rearrange("p (g t) -> p g t", t=T)
                    a = a[:, :, bass.ds(i * (RING * SET) + s * SET, SET)]
                    g = gp[:, s % 2, 0:SET * HALF].rearrange("p (t g) -> p g t", t=SET)
                    nc.vector.tensor_tensor(a, a, g, ALU.mult).then_inc(weighted, 1)

                dve.wait_ge(evac_act, 2 + layer * (16 + KEYS) + 16 + HALF)
                hots(0, 0, 0)
                with dve.Fori(0, HALF // RING - 1) as i:
                    for s in range(RING):
                        hots(0, i + (s + 1) // RING, (s + 1) % RING)
                        weigh(0, i, s)
                for s in range(RING):
                    if s + 1 < RING:
                        hots(0, HALF // RING - 1, s + 1)
                    weigh(0, HALF // RING - 1, s)

                n0 = AT[layer, "down"]

                def low_weight(g, s):
                    dve.wait_ge(wh_ready, g + (layer * KEYS + 1))
                    a = A[:, g * T:(g + 1) * T] if isinstance(g, int) else A[:, bass.ds(g * T, T)]
                    nc.vector.tensor_tensor(mov_l[:, s], a, mov_h[:, s].bitcast(F32),
                                            ALU.subtract).then_inc(wl_ready, 1)

                hots(1, 0, 0)
                for s in range(AHEAD):
                    low_weight(s, s)
                dve.wait_ge(evac_act, 2 + (layer + 1) * (16 + KEYS))
                with dve.Fori(0, HALF // RING - 1) as i:
                    for s in range(RING):
                        hots(1, i + (s + 1) // RING, (s + 1) % RING)
                        low_weight(i * RING + (s + AHEAD), (s + AHEAD) % RING)
                        weigh(1, i, s)
                last = HALF - RING
                for s in range(RING):
                    if s + 1 < RING:
                        hots(1, last // RING, s + 1)
                    if s + AHEAD < RING:
                        low_weight(last + s + AHEAD, (s + AHEAD) % RING)
                    weigh(1, last // RING, s)
                for s in range(AHEAD):
                    low_weight(HALF + s, s)
                if layer == 0:
                    nc.vector.memset(macc.rearrange("p m n -> p (m n)"), 0.0).then_inc(macc_done, 1)
                    dve.wait_ge(macc_done, 3)
                body = 8 if layer == 0 else RING

                def second(i, s, cut):
                    n = s + AHEAD
                    if not (cut and n >= body):
                        low_weight(i * body + (HALF + n), n % RING)
                    if layer == 0 and s < MODS:
                        dve.wait_ge(next_in[s], i * 16 + 16)
                        dve.wait_ge(next_used, i * MODS + (s + 1))
                        add_mod(s, ntile[:, s], i, False).then_inc(next_used, 1)

                with dve.Fori(0, HALF // body - 1) as i:
                    for s in range(body):
                        second(i, s, False)
                for s in range(body):
                    second(HALF // body - 1, s, True)
                dve.wait_ge(acc_done, layer + 1)
                dve.wait_ge(reloaded, 16 * (layer + 1))
                for c in range(DC):
                    nc.vector.scalar_tensor_tensor(X[:, c], acc[:, c // 2, (c % 2) * T:(c % 2 + 1) * T],
                                                   mod[:, 5 * DC + c:5 * DC + c + 1], X[:, c],
                                                   ALU.mult, ALU.add).then_inc(x_ready, 1)
            norm(4)

        @block.tensor
        def _(pe):
            pe.sem_inc(product, RING)
            pe.wait_ge(const_ready, 3)

            def sum_mod(ms, last=True):
                for m in ms:
                    for c in range(DC):
                        ins = nc.tensor.matmul(gp[:, 1, m * DC + c:m * DC + c + 1], macc[:, m, c * P:(c + 1) * P],
                                               ones[:, 0:1], start=True, stop=True)
                if last:
                    ins.then_inc(msum_done, 1)

            def stats(k):
                for c in range(DC):
                    pe.wait_ge(sq_done, DC * k + c + 1)
                    for tc in range(TC):
                        ins = nc.tensor.matmul(gp[:, 0, tc:tc + 1], sq[:, c, tc * P:(tc + 1) * P], ones[:, 0:1],
                                               start=(c == 0 and tc == 0), stop=(c == DC - 1),
                                               skip_group_check=True)
                ins.then_inc(stat_done, 1)
                for tc in range(TC):
                    pe.wait_ge(diag_done, TC * k + tc + 1)
                    ins = nc.tensor.matmul(gp[:, 0, T + tc * P:T + (tc + 1) * P], ones[:], diag[:, tc],
                                           start=True, stop=True)
                ins.then_inc(rs_done, 1)

            moved = [0]

            def moving(c, s):
                if s == 0:
                    pe.wait_ge(ml_done, moved[0] * DC + c + 1)

            def three(dst, s, c, mv, first, last, skip=False):
                for n, (w, m) in enumerate(((high, mov_h), (high, mov_l), (low, mov_h))):
                    ins = nc.tensor.matmul(dst, w[s][:, c], m[:, mv], start=(first and n == 0),
                                           stop=(last and n == 2), skip_group_check=skip)
                return ins

            def project(layer, name, i, s, evac, evac0):
                pe.wait_ge(low_ready, i * RING + (AT[layer, name] + s + 1))
                pe.wait_ge(evac, i * RING + (evac0 + s + 1))
                for c in range(DC):
                    moving(c, s)
                    ins = three(ps[:, s % 2, 0:T], s, c, c, c == 0, c == DC - 1)
                ins.then_inc(product, 1)

            def run(layer, name, tiles, evac, evac0):
                with pe.Fori(0, tiles // RING) as i:
                    for s in range(RING):
                        project(layer, name, i, s, evac, evac0)
                if name != "query":
                    moved[0] += 1

            for m in range(2):
                pe.wait_ge(macc_done, m + 1)
                sum_mod((m,), last=(m == 1))
            out_dve = 0
            for layer in range(LAYERS):
                out_act = layer * (16 + KEYS)
                if layer == 1:
                    pe.wait_ge(next_used, MODS + MODS * DC)
                    pe.wait_ge(weighted, 2 * HALF)
                    sum_mod(range(MODS))
                stats(2 * layer)
                if layer == 0:
                    run(0, "conv_in", 24, evac_dve, 0)
                    pe.wait_ge(mtile_used, 2 + 24)
                    sum_mod((2, 3, 4))
                    run(0, "conv_out", 8, evac_dve, 24)
                    pe.wait_ge(mtile_used, 2 + 32)
                    sum_mod((5,))
                    out_dve = 32
                else:
                    pe.wait_ge(evac_act, 2 + out_act)
                    run(1, "pool_in", 8, evac_dve, 32)
                    for s in range(RING):
                        pe.wait_ge(low_ready, AT[1, "pool_group"] + s + 1)
                        pe.wait_ge(evac_dve, 40 + s + 1)
                        for oc in range(2):
                            for kc in range(2):
                                pe.wait_ge(ml_done, moved[0] * DC + 2 * s + kc + 1)
                                ins = three(ps[:, s % 2, oc * T:(oc + 1) * T], s, 2 * oc + kc, 2 * s + kc,
                                            kc == 0, kc == 1)
                        ins.then_inc(product, 1)
                    moved[0] += 1
                    run(1, "pool_out", 8, evac_dve, 44)
                    out_dve = 52
                stats(2 * layer + 1)
                run(layer, "query", 16, evac_act, out_act)
                pe.wait_ge(evac_act, 2 + out_act + 16)
                pe.wait_ge(keys_in, 16 * (layer + 1))
                for n in range(8):
                    if n >= 2:
                        pe.wait_ge(score_out, 8 * layer + n - 1)
                    for q in range(4):
                        tc, hs = n // 4, 4 * (n % 4) + q
                        ins = nc.tensor.matmul(gp[:, n % 2, q * P:(q + 1) * P], Q[:, hs, tc * P:(tc + 1) * P],
                                               keys[:, hs % 2], start=True, stop=True)
                    ins.then_inc(score_done, 1)

                def ups(first):
                    n0 = AT[layer, "up"]
                    with pe.Fori(0, HALF // RING) as i:
                        for s in range(RING):
                            pe.wait_ge(low_ready, i * RING + (n0 + first + s + 1))
                            pe.wait_ge(evac_act, i * RING + (out_act + 16 + first + s + 1))
                            for c in range(DC):
                                ins = three(ps[:, s % 2, 0:T], s, c, c, c == 0, c == DC - 1)
                            ins.then_inc(product, 1)
                            if first:
                                scatter(0, i, s)

                def scatter(half, i, s):
                    k0 = (2 * layer + half) * HALF
                    pe.wait_ge(hot1_ready, i * RING + (k0 + s + 1))
                    for j in range(SET):
                        for n in range(PARTS):
                            ins = nc.tensor.matmul(gp[:, s % 2, j * HALF:(j + 1) * HALF], hot2[:, s % 2, j],
                                                   hot1[:, s % 2, n, j], start=(n == 0), stop=(n == PARTS - 1))
                    ins.then_inc(scattered, 1)

                ups(0)
                pe.wait_ge(pick_done, layer + 1)
                pe.wait_ge(score_out, 8 * (layer + 1))
                for dst, src in ((gp[:, 0, 0:T], EX[:, 0:T]), (gp[:, 0, T:2 * T], EX[:, T:2 * T]),
                                 (gp[:, 1, 0:T], GT)):
                    for tc in range(TC):
                        ins = nc.tensor.matmul(dst[:, tc * P:(tc + 1) * P], src[:, tc * P:(tc + 1) * P], eye,
                                               start=True, stop=True)
                ins.then_inc(turned, 1)
                pe.wait_ge(turned_out, 3 * (layer + 1))
                moved[0] += 1
                ups(HALF)

                if layer == 1:
                    pe.wait_ge(x_ready, DC)
                for b in range(4):
                    for q in range(4):
                        nc.tensor.matmul(acc[:, b, q * P:(q + 1) * P], zeros[:], zeros[:], start=(q == 0),
                                         stop=False, skip_group_check=True)
                n0 = AT[layer, "down"]
                for half in range(2):
                    with pe.Fori(0, HALF // RING) as i:
                        for s in range(RING):
                            if half == 0:
                                scatter(1, i, s)
                            pe.wait_ge(low_ready, i * RING + (n0 + half * HALF + s + 1))
                            pe.wait_ge(wl_ready, i * RING + (layer * KEYS + half * HALF + s + 1))
                            for c in range(DC):
                                ins = three(acc[:, c // 2, (c % 2) * T:(c % 2 + 1) * T], s, c, s, False, False, True)
                            ins.then_inc(product, 1)
                for b in range(4):
                    for q in range(4):
                        ins = nc.tensor.matmul(acc[:, b, q * P:(q + 1) * P], zeros[:], zeros[:], start=False,
                                               stop=(q == 3), skip_group_check=True)
                ins.then_inc(acc_done, 1)
            stats(4)


def kernel(**inputs):
    import numpy as np
    import concourse.bacc as bacc
    from concourse.bass_utils import run_bass_kernel_spmd

    a = {k: np.asarray(v) for k, v in inputs.items()}

    def chunks(v):
        v = v.reshape(-1, DC, P)
        return v.transpose(2, 0, 1).reshape(P, -1)

    def tiles(w):
        k, n = w.shape
        return w.reshape(k // P, P, n // P, P).transpose(2, 1, 0, 3).reshape(n // P, P, k)

    counts = np.array([[1.0 / min(t + 1, w) for t in range(PAD)] for w in WINDOWS], np.float32).reshape(1, -1)
    small = np.concatenate([
        chunks(a["c"]), chunks(a["norm1_g"]), chunks(a["norm2_g"]), chunks(a["b_mod"]), chunks(a["conv_w"]),
        chunks(a["pool_scale"]), chunks(a["final_g"]),
        np.broadcast_to(np.arange(P, dtype=np.float32), (P, P)), np.eye(P, dtype=np.float32),
        np.broadcast_to(counts, (P, counts.size))], axis=1)
    order = [g * DC + j for j in range(DC) for g in (1, 2, 0)]
    grp = a["pool_w_grp"][0].reshape(4, 2, P, 2, P).transpose(0, 2, 3, 1, 4).reshape(4, P, 4 * P)
    arrays = {
        "small": small,
        "x_t": a["x"][0].T.reshape(DC, P, T).transpose(1, 0, 2).reshape(P, DC * T),
        "k_t": np.stack([a["peer_k1"].transpose(0, 2, 1), a["peer_k2"].transpose(0, 2, 1)], axis=2),
        "w_mod": a["w_mod"],
        "conv_in": tiles(a["conv_w_in"][0])[order],
        "conv_out": tiles(a["conv_w_out"][0]),
        "query": np.stack([tiles(w) for w in a["peer_w_q"]]),
        "up": a["peer_u"].reshape(LAYERS, KEYS, P, DC, P).transpose(0, 1, 4, 3, 2).reshape(LAYERS, KEYS, P, D),
        "down": a["peer_v"].reshape(LAYERS, KEYS, P, D),
        "pool_in": tiles(a["pool_w_in"][0]),
        "pool_group": np.concatenate([grp, np.zeros_like(grp)], axis=2),
        "pool_out": tiles(a["pool_w_out"][0]),
    }
    nc = bacc.Bacc("TRN2", target_bir_lowering=False, num_devices=1)
    args = []
    for name, v in arrays.items():
        arrays[name] = v = np.ascontiguousarray(v)
        args.append(nc.dram_tensor(name, v.shape, mybir.dt.from_np(v.dtype), kind="ExternalInput").ap())
    x_spill = nc.dram_tensor("x_spill", (P, DC * T), F32, kind="Internal").ap()
    out = nc.dram_tensor("out", (P, DC * T), F32, kind="ExternalOutput").ap()
    program(nc, *args, x_spill, out)
    r = run_bass_kernel_spmd(nc, [arrays], core_ids=[0])
    got = np.asarray(r.results[0]["out"])
    return got.reshape(P, DC, T).transpose(2, 1, 0).reshape(1, T, D)
```

```python
from contextlib import ExitStack

import concourse.bass as bass
from concourse import mybir

F32 = mybir.dt.float32
F32R = mybir.dt.float32r
BF16 = mybir.dt.bfloat16
U32 = mybir.dt.uint32
ALU = mybir.AluOpType
ACT = mybir.ActivationFunctionType
AX_X = mybir.AxisListType.X

P = 128
D = 1024
DC = D // P
T = 256
TC = T // P
LAYERS = 2
NEXT = 5
MODS = 6
HEADS = 8
KEYS = 128
TOPK = 16
HALF = KEYS // 2
EPS = 1e-6
RING = 4
AHEAD = 3
WINDOWS = (16, 8, 4, 2)
PAD = max(WINDOWS)
TAPS = 3
SET = T // HALF
PARTS = 3
LOWEST = -3.0e38

C_C, C_N1, C_N2 = 0, 8, 24
C_BM = 40
C_CW = C_BM + LAYERS * MODS * DC
C_PS = C_CW + TAPS * DC
C_FG = C_PS + DC
C_IOTA = C_FG + DC
C_EYE = C_IOTA + P
C_CNT = C_EYE + P
SMALL = C_CNT + len(WINDOWS) * PAD

HEAD = [(1, 0, 1), (1, 1, 1), (1, 2, 2), (1, 4, 2), (1, 6, 2), (0, 0, 2), (0, 2, 2), (0, 4, 2), (0, 6, 1), (0, 7, 1)]
STREAM = [[("conv_in", 24), ("conv_out", 8), ("query", 16), ("up", KEYS), ("down", KEYS)],
          [("pool_in", 8), ("pool_group", 4), ("pool_out", 8), ("query", 16), ("up", KEYS), ("down", KEYS)]]


def places():
    at, n = {}, 0
    for layer, runs in enumerate(STREAM):
        for name, tiles in runs:
            at[layer, name] = n
            n += tiles
    return at, n


class Chain:

    def __init__(self, eng, sem):
        self.eng, self.sem, self.base, self.k, self.i, self.per = eng, sem, 0, 0, None, 0

    def value(self):
        return self.base + self.k if self.i is None else self.i * self.per + (self.base + self.k)

    def __call__(self, ins, met=None):
        self.k += 1
        ins.then_inc(self.sem, 1)
        value = self.value()
        if met is not None:
            self.eng.compute_val(value)
            self.eng.wait_ge(*met)
        self.eng.wait_ge(self.sem, value)

    def enter(self, i, per):
        self.base, self.k, self.i, self.per = self.base + self.k, 0, i, per

    def leave(self, trips):
        assert self.k == self.per, (self.k, self.per)
        self.base, self.k, self.i = self.base + self.per * trips, 0, None


def program(nc, small, x_in, k_t, w_mod, conv_in, conv_out, query, up, down, pool_in, pool_group, pool_out,
            x_spill, out):
    AT, TILES = places()
    tiles_of = {("conv_in", 0): conv_in, ("conv_out", 0): conv_out, ("pool_in", 1): pool_in,
                ("pool_group", 1): pool_group, ("pool_out", 1): pool_out}
    for layer in range(LAYERS):
        for name, src in (("query", query), ("up", up), ("down", down)):
            tiles_of[name, layer] = src[layer]

    with ExitStack() as ctx:
        def sb(name, shape, dt):
            return ctx.enter_context(nc.sbuf_tensor(name, shape, dt))

        def sem(name):
            return ctx.enter_context(nc.semaphore(name))

        A = sb("acts", [P, KEYS * T], F32)
        raw = sb("raw", [P, RING, D], F32)
        high = [sb(f"high{s}", [P, DC, P], F32R) for s in range(RING)]
        low = [sb(f"low{s}", [P, DC, P], F32R) for s in range(RING)]
        mov_h = sb("mov_h", [P, DC, T], F32R)
        mov_l = sb("mov_l", [P, DC, T], F32R)
        sm = sb("sm", [P, SMALL], F32)
        keys = sb("keys", [P, 2, P], F32)
        mod = sb("mod", [P, MODS * DC], F32)
        gs = sb("gs", [P, DC], F32)
        cact = sb("cact", [P, DC], F32)
        ctmp = sb("ctmp", [P, DC], F32)
        ones = sb("ones", [P, P], F32)
        eps = sb("eps", [P, 1], F32)
        warm = sb("warm", [P, 1], F32)
        zeros = sb("zeros", [P, P], BF16)
        idx1 = sb("idx1", [P, T], BF16)
        idx2 = sb("idx2", [P, T], BF16)
        gate = sb("gate", [P, PARTS, T], BF16)
        gate_rest = sb("gate_rest", [P, T], F32)
        eq1 = sb("eq1", [P, 2, SET, HALF], BF16)
        hot1 = sb("hot1", [P, 2, PARTS, SET, HALF], BF16)
        hot2 = sb("hot2", [P, 2, SET, P], BF16)

        iota = sm[:, C_IOTA:C_IOTA + P]
        eye = sm[:, C_EYE:C_EYE + P]

        def part(a, n):
            return A[:, a:a + n]

        X = part(0, DC * T).rearrange("p (c t) -> p c t", c=DC)
        mtile = part(2048, 2 * D).rearrange("p (s n) -> p s n", s=2)
        ntile = part(10240, NEXT * D).rearrange("p (s n) -> p s n", s=NEXT)
        macc = part(4096, MODS * D).rearrange("p (m n) -> p m n", m=MODS)
        B0 = HALF * T
        mhead = part(B0, 2 * DC * D).rearrange("p (m k n) -> p m k n", m=2, k=DC)
        xr = part(13312, DC * T).rearrange("p (c t) -> p c t", c=DC)
        SQ0 = 11264
        sq = part(SQ0, DC * T).rearrange("p (c t) -> p c t", c=DC)
        sd = part(10240, TC)
        rstd = part(10240 + TC, TC)
        total = part(10240 + 3 * T, T)
        diag = part(10240 + 2 * TC, T).rearrange("p (c t) -> p c t", c=TC)
        vp = part(B0, 2 * (T + 2)).rearrange("p (s t) -> p s t", s=2)
        cs = part(B0 + 1024, 2 * T).rearrange("p (s t) -> p s t", s=2)
        cv = part(B0 + 1536, 3 * T).rearrange("p (s t) -> p s t", s=3)
        Z = part(B0 + 2560, DC * T).rearrange("p (c t) -> p c t", c=DC)
        UP = part(B0 + 4864, DC * (PAD + T)).rearrange("p (c t) -> p c t", c=DC)
        W1 = part(B0 + 7168, 2 * (PAD + T)).rearrange("p (c t) -> p c t", c=2)
        W2 = part(B0 + 7936, 2 * (PAD + T)).rearrange("p (c t) -> p c t", c=2)
        WS = part(B0 + 8704, 2 * PAD).rearrange("p (c t) -> p c t", c=2)
        ROWS = TC * HEADS
        S = part(B0, ROWS * 2 * KEYS)
        Q = part(B0 + 8192, 2 * HEADS * T).rearrange("p (n t) -> p n t", n=2 * HEADS)
        EQ = part(B0 + 8192, T * TOPK)
        o = B0 + 12288
        SC = part(o, T)
        FL = part(o + 256, T).bitcast(U32)
        IDX = part(o + 512, 2 * T)
        ABu = part(o + 1024, 2 * T).bitcast(U32)
        AB = part(o + 1536, 2 * T)
        EX = part(o + 2048, 2 * T)
        GT = part(o + 2560, T)
        SUM = part(o + 2816, ROWS)
        RS = part(o + 2832, ROWS)
        s2 = part(o + 2848, 2 * KEYS).rearrange("p (s n) -> p s n", s=2)
        s3 = part(o + 3104, 2 * KEYS).rearrange("p (s n) -> p s n", s=2)
        v16 = part(o + 3360, 2 * TOPK).rearrange("p (s n) -> p s n", s=2)
        i16 = part(o + 3392, 2 * TOPK).rearrange("p (s n) -> p s n", s=2).bitcast(U32)
        cand = part(o + 3424, TOPK * TOPK)
        cand2 = part(o + 3680, TOPK * TOPK)
        b16 = part(o + 3936, TOPK)
        f16 = part(o + 3952, TOPK).bitcast(U32)

        def psum(name, n):
            return ctx.enter_context(nc.psum_tensor(name, [P, n, 512], F32))

        ps = psum("ps", 2)
        gp = psum("gp", 2)
        acc = psum("acc", 4)

        raw_full = [sem(f"raw_full{s}") for s in range(RING)]
        high_ready = sem("high_ready")
        low_ready = sem("low_ready")
        product = sem("product")
        evac_dve = sem("evac_dve")
        evac_act = sem("evac_act")
        small_in, x_in_s, keys_in = sem("small_in"), sem("x_in_s"), sem("keys_in")
        mhead_in = [sem(f"mhead_in{n}") for n in range(len(HEAD))]
        mtile_in = [sem(f"mtile_in{n}") for n in range(2)]
        shift2_in = [sem(f"shift2_in{n}") for n in range(2)]
        shift2_used = sem("shift2_used")
        mtile_used = sem("mtile_used")
        next_in = [sem(f"next_in{n}") for n in range(NEXT)]
        next_used = sem("next_used")
        macc_done = sem("macc_done")
        msum_done = sem("msum_done")
        mod_taken = sem("mod_taken")
        const_ready = sem("const_ready")
        cexp = sem("cexp")
        x_ready = sem("x_ready")
        warmed = sem("warmed")
        sq_done, stat_done, sd_done = sem("sq_done"), sem("stat_done"), sem("sd_done")
        xr_done, mh_done, ml_done = sem("xr_done"), sem("mh_done"), sem("ml_done")
        z_ready = sem("z_ready")
        score_done, score_out = sem("score_done"), sem("score_out")
        soft_in, soft_exp = sem("soft_in"), sem("soft_exp")
        pick_done, turned, turned_out = sem("pick_done"), sem("turned"), sem("turned_out")
        hot1_ready = sem("hot1_ready")
        hot_eq = sem("hot_eq")
        scattered, weighted = sem("scattered"), sem("weighted")
        wh_ready, wl_ready = sem("wh_ready"), sem("wl_ready")
        spilled, reloaded = sem("spilled"), sem("reloaded")
        acc_done = sem("acc_done")
        step = sem("step")
        diag_done, spread_done = sem("diag_done"), sem("spread_done")
        total_done = sem("total_done")
        stored = sem("stored")

        def tile_row(s):
            return raw[:, s]

        def flat(t):
            return t[:].rearrange("p a b -> p (a b)")

        block = ctx.enter_context(nc.Block())

        @block.sync
        def _(sp):
            sp.sem_inc(mtile_used, 2)
            sp.sem_inc(next_used, NEXT)
            sp.dma_start(sm[:], small).then_inc(small_in, 16)
            def load(layer, name, j, s):
                n0 = AT[layer, name]
                static = isinstance(j, int)
                if not (static and n0 + j < RING):
                    sp.wait_ge(low_ready, j + (n0 - RING + 1))
                src = tiles_of[name, layer]
                src = src[j] if static else src[bass.ds(j, 1)].rearrange("a p n -> (a p) n")
                sp.dma_start(tile_row(s), src).then_inc(raw_full[s], 16)

            def load_mod(layer, m, k, t, slot):
                sp.wait_ge(mtile_used, t + 1)
                sp.dma_start(mtile[:, slot], w_mod[layer, k * P:(k + 1) * P, m * D:(m + 1) * D]
                             ).then_inc(mtile_in[slot], 16)

            for n, (m, k, ks) in enumerate(HEAD):
                if n == 2:
                    sp.dma_start(A[:, 0:DC * T], x_in).then_inc(x_in_s, 16)
                if n == len(HEAD) - 2:
                    load(0, "conv_in", 0, 0)
                sp.dma_start(mhead[:, m, k:k + ks],
                             w_mod[0, k * P:(k + ks) * P, m * D:(m + 1) * D].rearrange("(k p) n -> p k n", p=P)
                             ).then_inc(mhead_in[n], 16)

            mods = [(m, k) for k in range(DC) for m in (2, 4)]
            behind = [3 + 3 * (u // 2) + 2 * (u % 2) for u in range(2 * DC)]
            shift2 = {10: 0, 18: 1, 24: 2, 25: 3, 27: 4, 28: 5, 30: 6, 31: 7}
            for t in range(1, 32):
                if t < 24:
                    load(0, "conv_in", t, t % RING)
                elif t < 32:
                    load(0, "conv_out", t - 24, t % RING)
                for u in range(2 * DC):
                    if behind[u] == t:
                        load_mod(0, *mods[u], u, u % 2)
                if t in shift2:
                    n = shift2[t]
                    sp.wait_ge(macc_done, 1)
                    if n >= 2:
                        sp.wait_ge(shift2_in[n % 2], (n // 2) * 16)
                    sp.dma_start(mhead[:, 1, n], w_mod[0, n * P:(n + 1) * P, 3 * D:4 * D]
                                 ).then_inc(shift2_in[n % 2], 16)

            def run(layer, name, tiles, first=0):
                with sp.Fori(0, tiles // RING) as i:
                    for s in range(RING):
                        load(layer, name, i * RING + (first + s), s)

            for layer in range(LAYERS):
                if layer == 1:
                    run(1, "pool_in", 8)
                    run(1, "pool_group", 4)
                    run(1, "pool_out", 8)
                with sp.Fori(0, 16 // RING) as i:
                    for s in range(RING):
                        load(layer, "query", i * RING + s, s)
                        if s % 2:
                            sp.wait_ge(mtile_used, i * 2 + ((2 + layer) * DC + s // 2 + 1))
                            w = w_mod[layer, :, 5 * D:6 * D].rearrange("(k p) n -> k p n", p=P)
                            sp.dma_start(mtile[:, s // 2], w[bass.ds(i * 2 + s // 2, 1)].rearrange("a p n -> (a p) n")
                                         ).then_inc(mtile_in[s // 2], 16)
                run(layer, "up", KEYS)
                if layer == 1:
                    run(1, "down", KEYS)
                else:
                    run(0, "down", HALF)
                    sp.wait_ge(wl_ready, HALF)
                    with sp.Fori(0, DC) as i:
                        for q in range(8):
                            load(0, "down", i * 8 + (HALF + q), q % RING)
                            if q < NEXT:
                                sp.wait_ge(next_used, i * NEXT + (q + 1))
                                w = w_mod[1, :, q * D:(q + 1) * D].rearrange("(k p) n -> k p n", p=P)
                                sp.dma_start(ntile[:, q], w[bass.ds(i, 1)].rearrange("a p n -> (a p) n")
                                             ).then_inc(next_in[q], 16)
            for n in range(4):
                sp.wait_ge(xr_done, 4 * DC + 2 * n + 2)
                sp.dma_start(out[:, 2 * n * T:(2 * n + 2) * T],
                             A[:, B0 + 2 * n * T:B0 + (2 * n + 2) * T]).then_inc(stored, 16)
            sp.wait_ge(stored, 4 * 16)

        @block.gpsimd
        def _(pool):
            nc.gpsimd.memset(ones[:], 1.0).then_inc(const_ready, 1)
            nc.gpsimd.memset(eps[:], EPS).then_inc(const_ready, 1)
            nc.gpsimd.memset(zeros[:], 0.0).then_inc(const_ready, 1)
            nc.gpsimd.memset(macc[:, 2:MODS].rearrange("p m n -> p (m n)"), 0.0).then_inc(const_ready, 1)
            with pool.Fori(0, TILES // RING) as i:
                for s in range(RING):
                    pool.wait_ge(high_ready, i * RING + (s + 1))
                    nc.gpsimd.tensor_tensor(flat(low[s]), tile_row(s), flat(high[s]).bitcast(F32),
                                            ALU.subtract).then_inc(low_ready, 1)

        @block.scalar
        def _(act):
            act.sem_inc(evac_act, 2)
            act.sem_inc(evac_dve, 2)

            def round_tile(n, s):
                act.wait_ge(product, n + 1)
                nc.scalar.activation(flat(high[s]), tile_row(s), ACT.Copy).then_inc(high_ready, 1)

            def arrived(k, s):
                act.wait_ge(raw_full[s], k * 16)

            def ahead(i, n0, s):
                t = s + AHEAD
                arrived(i + (n0 // RING + t // RING + 1), t % RING)
                round_tile(i * RING + (n0 + t), t % RING)

            def load_table():
                warm_count[0] += 1
                nc.scalar.activation(warm[:], eps[:], ACT.Sqrt).then_inc(warmed, 1)
                act.wait_ge(warmed, warm_count[0])

            warm_count = [0]

            def norm(k):
                if k % 2 == 0:
                    for c in range(DC):
                        if k == 0:
                            act.wait_ge(x_in_s, 16)
                        else:
                            act.wait_ge(x_ready, (k // 2 - 1) * DC + c + 1)
                        nc.scalar.activation(sq[:, c], X[:, c], ACT.Square).then_inc(sq_done, 1)
                else:
                    act.dma_start(x_spill, flat2(X)).then_inc(spilled, 16)
                act.wait_ge(stat_done, k + 1)
                nc.scalar.activation(sd, gp[:, 0, 0:TC], ACT.Sqrt, bias=eps[:, 0:1],
                                     scale=1.0 / D).then_inc(sd_done, 1)
                if k == 4:
                    return
                if k == 0:
                    for n in range(AHEAD):
                        arrived(1, n)
                        nc.scalar.activation(flat(high[n]), tile_row(n), ACT.Copy).then_inc(high_ready, 1)
                shift = mod[:, (3 * (k % 2)) * DC:(3 * (k % 2) + 1) * DC]
                act.wait_ge(mod_taken, (2, 4, 6, 7)[k])
                for c in range(DC):
                    act.wait_ge(xr_done, DC * k + c + 1)
                    nc.scalar.activation(mov_h[:, c], xr[:, c], ACT.Identity,
                                         bias=shift[:, c:c + 1]).then_inc(mh_done, 1)

            def flat2(v):
                return v.rearrange("p c t -> p (c t)")

            def split_z(n_products, ready):
                act.wait_ge(product, n_products + RING)
                for c in range(DC):
                    act.wait_ge(*ready(c))
                    nc.scalar.activation(mov_h[:, c], Z[:, c], ACT.Copy).then_inc(mh_done, 1)

            def only_round(n0, tiles):
                with act.Fori(0, tiles // RING) as i:
                    for s in range(RING):
                        ahead(i, n0, s)

            def round_and_square(n0, evac0):
                with act.Fori(0, DC // RING) as i:
                    for s in range(RING):
                        ahead(i, n0, s)
                        act.wait_ge(evac_dve, i * RING + (2 + evac0 + s + 1))
                        nc.scalar.activation(A[:, bass.ds(i * (RING * T) + (SQ0 + s * T), T)],
                                             A[:, bass.ds(i * (RING * T) + s * T, T)], ACT.Square
                                             ).then_inc(sq_done, 1)

            act.dma_start(keys[:], k_t[0]).then_inc(keys_in, 16)
            act.wait_ge(small_in, 16)
            nc.scalar.activation(ctmp[:], sm[:, C_C:C_C + DC], ACT.Exp, scale=-1.0).then_inc(cexp, 1)
            act.wait_ge(const_ready, 2)
            load_table()
            for layer in range(LAYERS):
                norm_k = 2 * layer
                norm(norm_k)
                if layer == 0:
                    only_round(AT[0, "conv_in"], 24)
                    split_z(AT[0, "conv_out"], lambda c: (evac_dve, 2 + 3 * (c + 1)))
                    round_and_square(AT[0, "conv_out"], 24)
                else:
                    only_round(AT[1, "pool_in"], 8)
                    split_z(AT[1, "pool_group"], lambda c: (z_ready, c + 1))
                    only_round(AT[1, "pool_group"], 4)
                    split_z(AT[1, "pool_out"], lambda c: (evac_dve, 2 + 32 + 8 + c // 2 + 1))
                    round_and_square(AT[1, "pool_out"], 44)
                norm(norm_k + 1)
                n0 = AT[layer, "query"]
                with act.Fori(0, 16 // RING) as i:
                    for s in range(RING):
                        ahead(i, n0, s)
                        act.wait_ge(product, i * RING + (n0 + s + 1 + RING))
                        nc.scalar.activation(A[:, bass.ds(i * (RING * T) + (B0 + 8192 + s * T), T)],
                                             ps[:, s % 2, 0:T], ACT.Copy).then_inc(evac_act, 1)
                act.wait_ge(spilled, 16 * (layer + 1))
                n0 = AT[layer, "up"]

                def gelus(first, trips):
                    with act.Fori(0, trips) as i:
                        for s in range(RING):
                            ahead(i, n0 + first, s)
                            act.wait_ge(product, i * RING + (n0 + first + s + 1 + RING))
                            nc.scalar.activation(A[:, bass.ds(i * (RING * T) + (first + s) * T, T)],
                                                 ps[:, s % 2, 0:T], ACT.Gelu).then_inc(evac_act, 1)

                gelus(0, HALF // RING - 4)
                act.wait_ge(soft_in, layer + 1)
                nc.scalar.activation(SC, SC, ACT.Exp).then_inc(soft_exp, 1)
                gelus(HALF - 4 * RING, 4)
                act.wait_ge(turned, layer + 1)
                if layer == 0:
                    act.dma_start(keys[:], k_t[1]).then_inc(keys_in, 16)
                gelus(HALF, HALF // RING)

                n0 = AT[layer, "down"]

                def weight(g, s):
                    nc.scalar.activation(mov_h[:, s], A[:, bass.ds(g * T, T)] if not isinstance(g, int)
                                         else A[:, g * T:(g + 1) * T], ACT.Copy).then_inc(wh_ready, 1)

                for half in range(2):
                    first = half * HALF
                    act.wait_ge(weighted, (2 * layer + half + 1) * HALF)
                    for s in range(AHEAD):
                        act.wait_ge(product, n0 + first + s + 1 + (RING - 1 - s if half == 0 else 0))
                        weight(first + s, s)
                    with act.Fori(0, HALF // RING - 1) as i:
                        for s in range(RING):
                            ahead(i, n0 + first, s)
                            weight(i * RING + (first + s + AHEAD), (s + AHEAD) % RING)
                    last = n0 + first + HALF - RING
                    if half == 1:
                        load_table()
                    for s in range(RING):
                        if last + s + AHEAD < TILES:
                            ahead(0, last, s)
                        if s + AHEAD < RING:
                            if last + s + AHEAD >= TILES:
                                act.wait_ge(product, last + s + AHEAD + 1)
                            weight(first + HALF - RING + s + AHEAD, (s + AHEAD) % RING)
                    if half == 0:
                        act.wait_ge(wl_ready, (2 * layer + 1) * HALF)
                        act.dma_start(A[:, 0:DC * T], x_spill).then_inc(reloaded, 16)
            norm(4)

        @block.vector
        def _(dve):
            link = Chain(dve, step)

            def turn(v, n):
                return v.rearrange("p (r n) -> p r n", n=n)

            dve.wait_ge(cexp, 1)
            link(nc.vector.tensor_scalar(ctmp[:], ctmp[:], 1.0, None, ALU.add))
            link(nc.vector.reciprocal(ctmp[:], ctmp[:]))
            link(nc.vector.tensor_tensor(cact[:], ctmp[:], sm[:, C_C:C_C + DC], ALU.mult))

            def add_mod(m, tile, k, first):
                c = cact[:, k:k + 1] if isinstance(k, int) else cact[:, bass.ds(k, 1)]
                if first:
                    return nc.vector.tensor_scalar(macc[:, m], tile, c, None, ALU.mult)
                return nc.vector.scalar_tensor_tensor(macc[:, m], tile, c, macc[:, m], ALU.mult, ALU.add)

            def head_mod(m):
                for n, (block_, k0, ks) in enumerate(HEAD):
                    if block_ == m:
                        dve.wait_ge(mhead_in[n], 16)
                        for k in range(k0, k0 + ks):
                            link(add_mod(m, mhead[:, m, k], k, k == 0))
                dve.sem_inc(macc_done, 1)

            sums = [0]

            def finish_mod(layer, ms):
                sums[0] += 1
                dve.wait_ge(msum_done, sums[0])
                for m in ms:
                    a, b = m * DC, (m + 1) * DC
                    bm = C_BM + layer * MODS * DC
                    ins = nc.vector.tensor_tensor(mod[:, a:b], gp[:, 1, a:b], sm[:, bm + a:bm + b], ALU.add)
                ins.then_inc(mod_taken, 1)
                dve.wait_ge(mod_taken, sums[0])

            def norm(k, shift_last=None):
                g0 = (C_N1, C_N2)[k % 2] + (k // 2) * DC
                if k == 0:
                    head_mod(1)
                dve.wait_ge(sd_done, k + 1)
                link(nc.vector.reciprocal(rstd, sd))
                for tc in range(TC):
                    nc.vector.tensor_scalar(diag[:, tc], eye, rstd[:, tc:tc + 1], None, ALU.mult
                                            ).then_inc(diag_done, 1)
                if k == 0:
                    head_mod(0)
                    finish_mod(0, (1,))
                if k < 4:
                    scale = mod[:, (3 * (k % 2) + 1) * DC:(3 * (k % 2) + 2) * DC]
                    link(nc.vector.scalar_tensor_tensor(gs[:], scale, 1.0, sm[:, g0:g0 + DC], ALU.add, ALU.mult))
                    weight = gs[:]
                else:
                    weight = sm[:, C_FG:C_FG + DC]
                dve.wait_ge(spread_done, k + 1)
                if k < 4:
                    shift = mod[:, (3 * (k % 2)) * DC:(3 * (k % 2) + 1) * DC]

                def scaled(c):
                    dst = xr[:, c] if k < 4 else A[:, B0 + c * T:B0 + (c + 1) * T]
                    nc.vector.scalar_tensor_tensor(dst, X[:, c], weight[:, c:c + 1], gp[:, 0, T:2 * T], ALU.mult,
                                                   ALU.mult).then_inc(xr_done, 1)

                def rest(c):
                    moved[0] += 1
                    dve.wait_ge(mh_done, moved[0])
                    nc.vector.scalar_tensor_tensor(mov_l[:, c], xr[:, c], shift[:, c:c + 1],
                                                   mov_h[:, c].bitcast(F32), ALU.add,
                                                   ALU.subtract).then_inc(ml_done, 1)

                lag = 4 if shift_last else 2
                for c in range(DC):
                    if shift_last and c == lag:
                        shift_last()
                    scaled(c)
                    if k < 4 and c >= lag:
                        rest(c - lag)
                if k < 4:
                    for c in range(DC - lag, DC):
                        rest(c)

            moved = [0]

            def split_z():
                for c in range(DC):
                    moved[0] += 1
                    dve.wait_ge(mh_done, moved[0])
                    nc.vector.tensor_tensor(mov_l[:, c], Z[:, c], mov_h[:, c].bitcast(F32),
                                            ALU.subtract).then_inc(ml_done, 1)

            def bank(n0, j, s):
                dve.wait_ge(product, j + (n0 + 1 + RING))
                return ps[:, s % 2, 0:T]

            def use_mtile(m, k, t, slot):
                dve.wait_ge(mtile_in[slot], t)
                add_mod(m, mtile[:, slot], k, False).then_inc(mtile_used, 1)

            def residual(n0, layer):
                t0 = layer * (DC - 1)

                def add_squares(c):
                    if c >= 2:
                        dve.wait_ge(total_done, t0 + c - 1)
                    dve.wait_ge(sq_done, (2 * layer + 1) * DC + c + 1)
                    nc.vector.tensor_tensor(total, sq[:, 0] if c == 1 else total, sq[:, c],
                                            ALU.add).then_inc(total_done, 1)

                for c in range(DC):
                    if layer == 0:
                        dve.wait_ge(shift2_in[c % 2], (c // 2 + 1) * 16)
                        if c:
                            dve.wait_ge(shift2_used, c)
                        add_mod(3, mhead[:, 1, c], c, c == 0).then_inc(shift2_used, 1)
                    if c >= 2:
                        add_squares(c - 1)
                    dve.wait_ge(product, n0 + c + 1 + RING)
                    nc.vector.scalar_tensor_tensor(X[:, c], ps[:, c % 2, 0:T], mod[:, 2 * DC + c:2 * DC + c + 1],
                                                   X[:, c], ALU.mult, ALU.add).then_inc(evac_dve, 1)
                add_squares(DC - 1)

            def picks(rows):
                met = (score_out, 1)
                for src, spare, vals, idx in rows:
                    ins = nc.vector.max(vals[:, 0:8], src)
                link(ins, met=met)
                for src, spare, vals, idx in rows:
                    nc.vector.max_index(idx[:, 0:8], vals[:, 0:8], src)
                    ins = nc.vector.match_replace(spare, vals[:, 0:8], src, LOWEST)
                link(ins, met=met)
                for src, spare, vals, idx in rows:
                    ins = nc.vector.max(vals[:, 8:16], spare)
                link(ins, met=met)
                for src, spare, vals, idx in rows:
                    ins = nc.vector.max_index(idx[:, 8:16], vals[:, 8:16], spare)
                return ins

            for layer in range(LAYERS):
                if layer == 0:
                    norm(0, lambda: finish_mod(0, (0,)))
                    n0 = AT[0, "conv_in"]
                    link(nc.vector.memset(vp, 0.0))
                    dve.wait_ge(const_ready, 4)
                    with dve.Fori(0, 4) as i:
                        link.enter(i, 6)
                        for q in range(2):
                            s = 3 * q
                            w = [sm[:, bass.ds(i * 2 + (C_CW + k * DC + q), 1)] for k in range(TAPS)]
                            z = A[:, bass.ds(i * (2 * T) + (B0 + 2560 + q * T), T)]
                            p = bank(n0, i * 6 + s, s)
                            nc.vector.tensor_copy(cs[:, q], p).then_inc(evac_dve, 1)
                            use_mtile(2, i * 2 + q, i * (2 * 16) + (q + 1) * 16, 0)
                            p = bank(n0, i * 6 + s + 1, s + 1)
                            dve.wait_ge(evac_dve, i * 6 + (2 + s + 1))
                            nc.vector.tensor_tensor(vp[:, q, 2:2 + T], p, cs[:, q], ALU.mult).then_inc(evac_dve, 1)
                            dve.wait_ge(evac_dve, i * 6 + (2 + s + 2))
                            link(nc.vector.tensor_scalar(cv[:, 0], vp[:, q, 0:T], w[0], None, ALU.mult))
                            link(nc.vector.scalar_tensor_tensor(cv[:, 1], vp[:, q, 1:1 + T], w[1], cv[:, 0],
                                                                ALU.mult, ALU.add))
                            link(nc.vector.scalar_tensor_tensor(cv[:, 2], vp[:, q, 2:2 + T], w[2], cv[:, 1],
                                                                ALU.mult, ALU.add))
                            p = bank(n0, i * 6 + s + 2, s + 2)
                            nc.vector.tensor_tensor(z, p, cv[:, 2], ALU.mult).then_inc(evac_dve, 1)
                            use_mtile(4, i * 2 + q, i * (2 * 16) + (q + 1) * 16, 1)
                            dve.wait_ge(mtile_used, i * 4 + (2 + 2 * q + 2))
                        link.leave(4)
                    split_z()
                    finish_mod(0, (2,))
                    residual(AT[0, "conv_out"], 0)
                    finish_mod(0, (3, 4))
                    norm(1)
                else:
                    dve.wait_ge(x_ready, DC)
                    finish_mod(1, (0, 1))
                    norm(2)
                    n0 = AT[1, "pool_in"]
                    link(nc.vector.memset(UP[:, :, 0:PAD], 0.0))
                    for g, w in enumerate(WINDOWS):
                        for j in (2 * g, 2 * g + 1):
                            p = bank(n0, j, j)
                            nc.vector.tensor_copy(UP[:, j, PAD:PAD + T], p).then_inc(evac_dve, 1)
                        dve.wait_ge(evac_dve, 2 + 32 + 2 * g + 2)
                        src, span, spare = UP[:, 2 * g:2 * g + 2], 1, [W1, W2]
                        end = PAD + T
                        while span < w:
                            dst = spare[0]
                            lo = 2 * span - 1
                            link(nc.vector.tensor_tensor(dst[:, :, lo:end], src[:, :, lo:end],
                                                         src[:, :, lo - span:end - span], ALU.add))
                            src, span, spare = dst, 2 * span, spare[::-1]
                        u = UP[:, 2 * g:2 * g + 2]
                        z = Z[:, 2 * g:2 * g + 2]
                        counts = sm[:, C_CNT + g * PAD:C_CNT + (g + 1) * PAD].unsqueeze(1).broadcast_to([P, 2, PAD])
                        link(nc.vector.tensor_tensor(WS, src[:, :, PAD:2 * PAD], counts, ALU.mult))
                        link(nc.vector.scalar_tensor_tensor(z, src[:, :, PAD:end], 1.0 / w, u[:, :, PAD:end],
                                                            ALU.mult, ALU.subtract))
                        nc.vector.tensor_tensor(z[:, :, 0:PAD], WS, u[:, :, PAD:2 * PAD],
                                                ALU.subtract).then_inc(z_ready, 2)
                    split_z()
                    finish_mod(1, (2, 3))
                    n0 = AT[1, "pool_group"]
                    for j in range(4):
                        dve.wait_ge(product, n0 + j + 1 + RING)
                        for c in range(2):
                            ins = nc.vector.tensor_scalar(Z[:, 2 * j + c], ps[:, j % 2, c * T:(c + 1) * T],
                                                          sm[:, C_PS + 2 * j + c:C_PS + 2 * j + c + 1], None, ALU.mult)
                        ins.then_inc(evac_dve, 1)
                    split_z()
                    finish_mod(1, (4,))
                    residual(AT[1, "pool_out"], 1)
                    norm(3)
                for k in range(DC):
                    t = (2 + layer) * DC + k
                    dve.wait_ge(mtile_in[k % 2], (t // 2 + 1) * 16)
                    add_mod(5, mtile[:, k % 2], k, k == 0).then_inc(mtile_used, 1)
                    dve.wait_ge(mtile_used, 2 + t + 1)
                finish_mod(layer, (5,))

                for n in range(8):
                    dve.wait_ge(score_done, 8 * layer + n + 1)
                    nc.vector.tensor_copy(S[:, n * 512:(n + 1) * 512], gp[:, n % 2, :]).then_inc(score_out, 1)
                dve.wait_ge(score_out, 8 * (layer + 1))
                with dve.Fori(0, ROWS) as i:
                    link.enter(i, 10)
                    link(nc.vector.tensor_copy(s2.rearrange("p s n -> p (s n)"),
                                               A[:, bass.ds(i * (2 * KEYS) + B0, 2 * KEYS)]), met=(score_out, 1))
                    picks([(s2[:, side], s3[:, side], v16[:, side], i16[:, side]) for side in range(2)])
                    link(nc.vector.tensor_tensor(cand.rearrange("p (a b) -> p a b", a=TOPK),
                                                 v16[:, 0].unsqueeze(2).broadcast_to([P, TOPK, TOPK]),
                                                 v16[:, 1].unsqueeze(1).broadcast_to([P, TOPK, TOPK]), ALU.add),
                         met=(score_out, 1))
                    link(picks([(cand, cand2, b16, f16)]))
                    nc.vector.tensor_copy(A[:, bass.ds(i * TOPK + o, TOPK)], b16)
                    nc.vector.tensor_copy(A[:, bass.ds(i * TOPK + (o + 256), TOPK)].bitcast(U32), f16)
                    link(nc.vector.tensor_copy(A[:, bass.ds(i * (2 * TOPK) + (o + 512), 2 * TOPK)],
                                               i16.rearrange("p s n -> p (s n)")))
                    link.leave(ROWS)
                sc3 = turn(SC, TOPK)
                link(nc.vector.tensor_copy(RS, sc3[:, :, 0]))
                nc.vector.tensor_tensor(sc3, sc3, RS.unsqueeze(2).broadcast_to([P, ROWS, TOPK]),
                                        ALU.subtract).then_inc(soft_in, 1)
                nc.vector.tensor_scalar(ABu[:, 0:T], FL, 4, None, ALU.logical_shift_right)
                link(nc.vector.tensor_scalar(ABu[:, T:2 * T], FL, TOPK - 1, None, ALU.bitwise_and))
                link(nc.vector.tensor_copy(AB, ABu))
                idx4 = IDX.rearrange("p (r s n) -> p r s n", s=2, n=TOPK)
                for side in range(2):
                    eq = EQ.rearrange("p (r k) -> p r k", k=TOPK)
                    link(nc.vector.tensor_tensor(eq, AB[:, side * T:(side + 1) * T].unsqueeze(2)
                                                 .broadcast_to([P, T, TOPK]),
                                                 iota[:, 0:TOPK].unsqueeze(1).broadcast_to([P, T, TOPK]),
                                                 ALU.is_equal))
                    eq4 = EQ.rearrange("p (r k n) -> p r k n", k=TOPK, n=TOPK)
                    link(nc.vector.tensor_tensor(eq4, eq4, idx4[:, :, side].unsqueeze(2)
                                                 .broadcast_to([P, ROWS, TOPK, TOPK]), ALU.mult))
                    link(nc.vector.tensor_reduce(EX[:, side * T:(side + 1) * T], eq, AX_X, ALU.add))
                dve.wait_ge(soft_exp, layer + 1)
                link(nc.vector.tensor_reduce(SUM, sc3, AX_X, ALU.add))
                link(nc.vector.reciprocal(RS, SUM))
                nc.vector.tensor_tensor(turn(GT, TOPK), sc3, RS.unsqueeze(2).broadcast_to([P, ROWS, TOPK]),
                                        ALU.mult).then_inc(pick_done, 1)
                dve.wait_ge(turned, layer + 1)
                nc.vector.tensor_copy(idx1[:], gp[:, 0, 0:T]).then_inc(turned_out, 1)
                nc.vector.tensor_copy(idx2[:], gp[:, 0, T:2 * T]).then_inc(turned_out, 1)
                link(nc.vector.tensor_copy(gate[:, 0], gp[:, 1, 0:T]))
                nc.vector.tensor_tensor(gate_rest[:], gp[:, 1, 0:T], gate[:, 0], ALU.subtract).then_inc(turned_out, 1)
                dve.wait_ge(turned_out, 3 * (layer + 1))
                link(nc.vector.tensor_copy(gate[:, 1], gate_rest[:]))
                link(nc.vector.tensor_tensor(gate_rest[:], gate_rest[:], gate[:, 1], ALU.subtract))
                link(nc.vector.tensor_copy(gate[:, 2], gate_rest[:]))

                def hots(half, i, s):
                    def over(v, n):
                        v = v[:, bass.ds(i * (RING * SET) + s * SET, SET)]
                        return v.unsqueeze(2).broadcast_to([P, SET, n])

                    def number(a, b):
                        return iota[:, a:b].unsqueeze(1).broadcast_to([P, SET, b - a])

                    k0 = (2 * layer + half) * HALF
                    nc.vector.tensor_tensor(eq1[:, s % 2], number(half * HALF, (half + 1) * HALF), over(idx1, HALF),
                                            ALU.is_equal).then_inc(hot_eq, 1)
                    nc.vector.tensor_tensor(hot2[:, s % 2], number(0, P), over(idx2, P), ALU.is_equal)
                    dve.wait_ge(hot_eq, i * RING + (k0 + s + 1))
                    g = gate[:, :, bass.ds(i * (RING * SET) + s * SET, SET)]
                    nc.vector.tensor_tensor(hot1[:, s % 2],
                                            eq1[:, s % 2].unsqueeze(1).broadcast_to([P, PARTS, SET, HALF]),
                                            g.unsqueeze(3).broadcast_to([P, PARTS, SET, HALF]), ALU.mult
                                            ).then_inc(hot1_ready, 1)

                def weigh(half, i, s):
                    k0 = (2 * layer + half) * HALF
                    dve.wait_ge(scattered, i * RING + (k0 + s + 1))
                    a = A[:, half * B0:half * B0 + HALF * T].rearrange("p (g t) -> p g t", t=T)
                    a = a[:, :, bass.ds(i * (RING * SET) + s * SET, SET)]
                    g = gp[:, s % 2, 0:SET * HALF].rearrange("p (t g) -> p g t", t=SET)
                    nc.vector.tensor_tensor(a, a, g, ALU.mult).then_inc(weighted, 1)

                dve.wait_ge(evac_act, 2 + layer * (16 + KEYS) + 16 + HALF)
                hots(0, 0, 0)
                with dve.Fori(0, HALF // RING - 1) as i:
                    for s in range(RING):
                        hots(0, i + (s + 1) // RING, (s + 1) % RING)
                        weigh(0, i, s)
                for s in range(RING):
                    if s + 1 < RING:
                        hots(0, HALF // RING - 1, s + 1)
                    weigh(0, HALF // RING - 1, s)

                n0 = AT[layer, "down"]

                def low_weight(g, s):
                    dve.wait_ge(wh_ready, g + (layer * KEYS + 1))
                    a = A[:, g * T:(g + 1) * T] if isinstance(g, int) else A[:, bass.ds(g * T, T)]
                    nc.vector.tensor_tensor(mov_l[:, s], a, mov_h[:, s].bitcast(F32),
                                            ALU.subtract).then_inc(wl_ready, 1)

                hots(1, 0, 0)
                for s in range(AHEAD):
                    low_weight(s, s)
                dve.wait_ge(evac_act, 2 + (layer + 1) * (16 + KEYS))
                with dve.Fori(0, HALF // RING - 1) as i:
                    for s in range(RING):
                        hots(1, i + (s + 1) // RING, (s + 1) % RING)
                        low_weight(i * RING + (s + AHEAD), (s + AHEAD) % RING)
                        weigh(1, i, s)
                last = HALF - RING
                for s in range(RING):
                    if s + 1 < RING:
                        hots(1, last // RING, s + 1)
                    if s + AHEAD < RING:
                        low_weight(last + s + AHEAD, (s + AHEAD) % RING)
                    weigh(1, last // RING, s)
                for s in range(AHEAD):
                    low_weight(HALF + s, s)
                body = 8 if layer == 0 else RING

                def second(i, s, cut):
                    n = s + AHEAD
                    if not (cut and n >= body):
                        low_weight(i * body + (HALF + n), n % RING)
                    if layer == 0 and s < NEXT:
                        dve.wait_ge(next_in[s], i * 16 + 16)
                        first = isinstance(i, int) and i == 0
                        if not first:
                            dve.wait_ge(next_used, i * NEXT + (s + 1))
                        add_mod(s, ntile[:, s], i, first).then_inc(next_used, 1)

                for s in range(body):
                    second(0, s, False)
                with dve.Fori(0, HALF // body - 2) as i:
                    for s in range(body):
                        second(i + 1, s, False)
                for s in range(body):
                    second(HALF // body - 1, s, True)
                dve.wait_ge(reloaded, 16 * (layer + 1))
                for c in range(DC):
                    if c % 2 == 0 and c < DC - 2:
                        dve.wait_ge(acc_done, 3 * layer + c // 2 + 1)
                    elif c % 2 == 0:
                        dve.wait_ge(product, n0 + KEYS + RING)
                    nc.vector.scalar_tensor_tensor(X[:, c], acc[:, c // 2, (c % 2) * T:(c % 2 + 1) * T],
                                                   mod[:, 5 * DC + c:5 * DC + c + 1], X[:, c],
                                                   ALU.mult, ALU.add).then_inc(x_ready, 1)
            norm(4)

        @block.tensor
        def _(pe):
            pe.sem_inc(product, RING)
            pe.wait_ge(const_ready, 3)

            sums = [0]

            def sum_mod(ms):
                if sums[0]:
                    pe.wait_ge(mod_taken, sums[0])
                sums[0] += 1
                for m in ms:
                    for c in range(DC):
                        ins = nc.tensor.matmul(gp[:, 1, m * DC + c:m * DC + c + 1], macc[:, m, c * P:(c + 1) * P],
                                               ones[:, 0:1], start=True, stop=True)
                ins.then_inc(msum_done, 1)

            def token_sums(k, parts):
                for n, (sem_, value, src) in enumerate(parts):
                    pe.wait_ge(sem_, value)
                    for tc in range(TC):
                        ins = nc.tensor.matmul(gp[:, 0, tc:tc + 1], src[:, tc * P:(tc + 1) * P], ones[:, 0:1],
                                               start=(n == 0 and tc == 0), stop=(n == len(parts) - 1),
                                               skip_group_check=True)
                ins.then_inc(stat_done, 1)

            def square_sums(k):
                if k % 2:
                    token_sums(k, [(total_done, (k // 2 + 1) * (DC - 1), total)])
                else:
                    token_sums(k, [(sq_done, DC * k + c + 1, sq[:, c]) for c in range(DC)])

            def spread(k):
                for tc in range(TC):
                    pe.wait_ge(diag_done, TC * k + tc + 1)
                    ins = nc.tensor.matmul(gp[:, 0, T + tc * P:T + (tc + 1) * P], ones[:], diag[:, tc],
                                           start=True, stop=True)
                ins.then_inc(spread_done, 1)

            moved = [0]

            def moving(c):
                pe.wait_ge(ml_done, moved[0] * DC + c + 1)

            def three(dst, s, c, mv, first, last, skip=False):
                for n, (w, m) in enumerate(((high, mov_h), (high, mov_l), (low, mov_h))):
                    ins = nc.tensor.matmul(dst, w[s][:, c], m[:, mv], start=(first and n == 0),
                                           stop=(last and n == 2), skip_group_check=skip)
                return ins

            def project(layer, name, i, s, evac, evac0):
                pe.wait_ge(low_ready, i * RING + (AT[layer, name] + s + 1))
                pe.wait_ge(evac, i * RING + (evac0 + s + 1))
                for c in range(DC):
                    if s == 0:
                        moving(c)
                    ins = three(ps[:, s % 2, 0:T], s, c, c, c == 0, c == DC - 1)
                ins.then_inc(product, 1)

            def run(layer, name, tiles, evac, evac0):
                with pe.Fori(0, tiles // RING) as i:
                    for s in range(RING):
                        project(layer, name, i, s, evac, evac0)
                if name != "query":
                    moved[0] += 1

            for layer in range(LAYERS):
                out_act = layer * (16 + KEYS)
                if layer == 1:
                    pe.wait_ge(weighted, 2 * HALF)
                square_sums(2 * layer)
                if layer == 0:
                    pe.wait_ge(macc_done, 1)
                    sum_mod((1,))
                spread(2 * layer)
                if layer == 0:
                    pe.wait_ge(macc_done, 2)
                    sum_mod((0,))
                if layer == 0:
                    run(0, "conv_in", 24, evac_dve, 0)
                    pe.wait_ge(mtile_used, 2 + 2 * DC)
                    sum_mod((2,))
                    run(0, "conv_out", 8, evac_dve, 24)
                    pe.wait_ge(shift2_used, DC)
                    sum_mod((3, 4))
                    square_sums(1)
                else:
                    pe.wait_ge(evac_act, 2 + out_act)
                    run(1, "pool_in", 8, evac_dve, 32)
                    sum_mod((2, 3))
                    for s in range(RING):
                        pe.wait_ge(low_ready, AT[1, "pool_group"] + s + 1)
                        pe.wait_ge(evac_dve, 40 + s + 1)
                        for oc in range(2):
                            for kc in range(2):
                                pe.wait_ge(ml_done, moved[0] * DC + 2 * s + kc + 1)
                                ins = three(ps[:, s % 2, oc * T:(oc + 1) * T], s, 2 * oc + kc, 2 * s + kc,
                                            kc == 0, kc == 1)
                        ins.then_inc(product, 1)
                    moved[0] += 1
                    sum_mod((4,))
                    run(1, "pool_out", 8, evac_dve, 44)
                    square_sums(3)
                spread(2 * layer + 1)
                run(layer, "query", 16, evac_act, out_act)
                pe.wait_ge(mtile_used, 2 + (3 + layer) * DC)
                sum_mod((5,))
                pe.wait_ge(evac_act, 2 + out_act + 16)
                pe.wait_ge(keys_in, 16 * (layer + 1))
                for n in range(8):
                    if n == 1:
                        pe.wait_ge(mod_taken, sums[0])
                    elif n >= 2:
                        pe.wait_ge(score_out, 8 * layer + n - 1)
                    for q in range(4):
                        tc, hs = n // 4, 4 * (n % 4) + q
                        ins = nc.tensor.matmul(gp[:, n % 2, q * P:(q + 1) * P], Q[:, hs, tc * P:(tc + 1) * P],
                                               keys[:, hs % 2], start=True, stop=True)
                    ins.then_inc(score_done, 1)

                def ups(first):
                    n0 = AT[layer, "up"]
                    with pe.Fori(0, HALF // RING) as i:
                        for s in range(RING):
                            pe.wait_ge(low_ready, i * RING + (n0 + first + s + 1))
                            pe.wait_ge(evac_act, i * RING + (out_act + 16 + first + s + 1))
                            for c in range(DC):
                                ins = three(ps[:, s % 2, 0:T], s, c, c, c == 0, c == DC - 1)
                            ins.then_inc(product, 1)
                            if first:
                                scatter(0, i, s)

                def scatter(half, i, s):
                    k0 = (2 * layer + half) * HALF
                    pe.wait_ge(hot1_ready, i * RING + (k0 + s + 1))
                    for j in range(SET):
                        for n in range(PARTS):
                            ins = nc.tensor.matmul(gp[:, s % 2, j * HALF:(j + 1) * HALF], hot2[:, s % 2, j],
                                                   hot1[:, s % 2, n, j], start=(n == 0), stop=(n == PARTS - 1))
                    ins.then_inc(scattered, 1)

                ups(0)
                pe.wait_ge(pick_done, layer + 1)
                pe.wait_ge(score_out, 8 * (layer + 1))
                for dst, src in ((gp[:, 0, 0:T], EX[:, 0:T]), (gp[:, 0, T:2 * T], EX[:, T:2 * T]),
                                 (gp[:, 1, 0:T], GT)):
                    for tc in range(TC):
                        ins = nc.tensor.matmul(dst[:, tc * P:(tc + 1) * P], src[:, tc * P:(tc + 1) * P], eye,
                                               start=True, stop=True)
                ins.then_inc(turned, 1)
                pe.wait_ge(turned_out, 3 * (layer + 1))
                moved[0] += 1
                ups(HALF)

                if layer == 1:
                    pe.wait_ge(x_ready, DC)
                for b in range(4):
                    for q in range(4):
                        nc.tensor.matmul(acc[:, b, q * P:(q + 1) * P], zeros[:], zeros[:], start=(q == 0),
                                         stop=False, skip_group_check=True)
                n0 = AT[layer, "down"]
                for half in range(2):
                    def down_tile(i, s, closing):
                        pe.wait_ge(low_ready, i * RING + (n0 + half * HALF + s + 1))
                        pe.wait_ge(wl_ready, i * RING + (layer * KEYS + half * HALF + s + 1))
                        for c in range(DC):
                            ins = three(acc[:, c // 2, (c % 2) * T:(c % 2 + 1) * T], s, c, s, False, closing, True)
                            if closing and c % 2 and c < DC - 1:
                                ins.then_inc(acc_done, 1)
                        ins.then_inc(product, 1)

                    if half == 0:
                        with pe.Fori(0, HALF // RING) as i:
                            for s in range(RING):
                                scatter(1, i, s)
                                down_tile(i, s, False)
                    else:
                        with pe.Fori(0, HALF // RING - 1) as i:
                            for s in range(RING):
                                down_tile(i, s, False)
                        for s in range(RING):
                            if layer == 0 and s == RING - 1:
                                pe.wait_ge(next_used, NEXT + NEXT * DC)
                                pe.wait_ge(weighted, 2 * HALF)
                                sum_mod((0, 1))
                            down_tile(HALF // RING - 1, s, s == RING - 1)
            square_sums(4)
            spread(4)


def kernel(**inputs):
    import numpy as np
    import concourse.bacc as bacc
    from concourse.bass_utils import run_bass_kernel_spmd

    a = {k: np.asarray(v) for k, v in inputs.items()}

    def chunks(v):
        v = v.reshape(-1, DC, P)
        return v.transpose(2, 0, 1).reshape(P, -1)

    def tiles(w):
        k, n = w.shape
        return w.reshape(k // P, P, n // P, P).transpose(2, 1, 0, 3).reshape(n // P, P, k)

    groups = len(WINDOWS)
    pool_in = tiles(a["pool_w_in"][0]).reshape(groups, -1, P, D)[::-1].reshape(DC, P, D)
    pool_scale = a["pool_scale"].reshape(groups, -1)[::-1].reshape(1, D)
    pool_out = a["pool_w_out"][0].reshape(groups, -1, D)[::-1].reshape(D, D)
    counts = np.array([[1.0 / min(t + 1, w) for t in range(PAD)] for w in WINDOWS], np.float32).reshape(1, -1)
    small = np.concatenate([
        chunks(a["c"]), chunks(a["norm1_g"]), chunks(a["norm2_g"]), chunks(a["b_mod"]), chunks(a["conv_w"]),
        chunks(pool_scale), chunks(a["final_g"]),
        np.broadcast_to(np.arange(P, dtype=np.float32), (P, P)), np.eye(P, dtype=np.float32),
        np.broadcast_to(counts, (P, counts.size))], axis=1)
    order = [g * DC + j for j in range(DC) for g in (1, 2, 0)]
    grp = a["pool_w_grp"][0][::-1].reshape(4, 2, P, 2, P).transpose(0, 2, 3, 1, 4).reshape(4, P, 4 * P)
    arrays = {
        "small": small,
        "x_t": a["x"][0].T.reshape(DC, P, T).transpose(1, 0, 2).reshape(P, DC * T),
        "k_t": np.stack([a["peer_k1"].transpose(0, 2, 1), a["peer_k2"].transpose(0, 2, 1)], axis=2),
        "w_mod": a["w_mod"],
        "conv_in": tiles(a["conv_w_in"][0])[order],
        "conv_out": tiles(a["conv_w_out"][0]),
        "query": np.stack([tiles(w) for w in a["peer_w_q"]]),
        "up": a["peer_u"].reshape(LAYERS, KEYS, P, DC, P).transpose(0, 1, 4, 3, 2).reshape(LAYERS, KEYS, P, D),
        "down": a["peer_v"].reshape(LAYERS, KEYS, P, D),
        "pool_in": pool_in,
        "pool_group": np.concatenate([grp, np.zeros_like(grp)], axis=2),
        "pool_out": tiles(pool_out),
    }
    nc = bacc.Bacc("TRN2", target_bir_lowering=False, num_devices=1)
    args = []
    for name, v in arrays.items():
        arrays[name] = v = np.ascontiguousarray(v)
        args.append(nc.dram_tensor(name, v.shape, mybir.dt.from_np(v.dtype), kind="ExternalInput").ap())
    x_spill = nc.dram_tensor("x_spill", (P, DC * T), F32, kind="Internal").ap()
    out = nc.dram_tensor("out", (P, DC * T), F32, kind="ExternalOutput").ap()
    program(nc, *args, x_spill, out)
    r = run_bass_kernel_spmd(nc, [arrays], core_ids=[0])
    got = np.asarray(r.results[0]["out"])
    return got.reshape(P, DC, T).transpose(2, 1, 0).reshape(1, T, D)
```

```python
from contextlib import ExitStack

import concourse.bass as bass
from concourse import mybir

F32 = mybir.dt.float32
F32R = mybir.dt.float32r
BF16 = mybir.dt.bfloat16
U32 = mybir.dt.uint32
ALU = mybir.AluOpType
ACT = mybir.ActivationFunctionType
AX_X = mybir.AxisListType.X

P = 128
D = 1024
DC = D // P
T = 256
TC = T // P
LAYERS = 2
NEXT = 5
MODS = 6
HEADS = 8
KEYS = 128
TOPK = 16
HALF = KEYS // 2
EPS = 1e-6
RING = 4
AHEAD = 3
WINDOWS = (16, 8, 4, 2)
PAD = max(WINDOWS)
TAPS = 3
SETS = HALF // 2
SET = T // SETS
PARTS = 3
LOWEST = -3.0e38

C_C, C_N1, C_N2 = 0, 8, 24
C_BM = 40
C_CW = C_BM + LAYERS * MODS * DC
C_PS = C_CW + TAPS * DC
C_FG = C_PS + DC
C_IOTA = C_FG + DC
C_EYE = C_IOTA + P
C_CNT = C_EYE + P
SMALL = C_CNT + len(WINDOWS) * PAD

HEAD = [(1, 0, 1), (1, 1, 1), (1, 2, 2), (1, 4, 2), (1, 6, 2), (0, 0, 2), (0, 2, 2), (0, 4, 2), (0, 6, 1), (0, 7, 1)]
STREAM = [[("conv_in", 24), ("conv_out", 8), ("query", 16), ("up", KEYS), ("down", KEYS)],
          [("pool_in", 8), ("pool_group", 4), ("pool_out", 8), ("query", 16), ("up", KEYS), ("down", KEYS)]]


def places():
    at, n = {}, 0
    for layer, runs in enumerate(STREAM):
        for name, tiles in runs:
            at[layer, name] = n
            n += tiles
    return at, n


class Chain:

    def __init__(self, eng, sem):
        self.eng, self.sem, self.base, self.k, self.i, self.per = eng, sem, 0, 0, None, 0

    def value(self):
        return self.base + self.k if self.i is None else self.i * self.per + (self.base + self.k)

    def __call__(self, ins, met=None):
        self.k += 1
        ins.then_inc(self.sem, 1)
        value = self.value()
        if met is not None:
            self.eng.compute_val(value)
            self.eng.wait_ge(*met)
        self.eng.wait_ge(self.sem, value)

    def enter(self, i, per):
        self.base, self.k, self.i, self.per = self.base + self.k, 0, i, per

    def leave(self, trips):
        assert self.k == self.per, (self.k, self.per)
        self.base, self.k, self.i = self.base + self.per * trips, 0, None


def program(nc, small, x_in, k_t, w_mod, conv_in, conv_out, query, up, down, pool_in, pool_group, pool_out,
            x_spill, out):
    AT, TILES = places()
    tiles_of = {("conv_in", 0): conv_in, ("conv_out", 0): conv_out, ("pool_in", 1): pool_in,
                ("pool_group", 1): pool_group, ("pool_out", 1): pool_out}
    for layer in range(LAYERS):
        for name, src in (("query", query), ("up", up), ("down", down)):
            tiles_of[name, layer] = src[layer]

    with ExitStack() as ctx:
        def sb(name, shape, dt):
            return ctx.enter_context(nc.sbuf_tensor(name, shape, dt))

        def sem(name):
            return ctx.enter_context(nc.semaphore(name))

        A = sb("acts", [P, KEYS * T], F32)
        raw = sb("raw", [P, RING, D], F32)
        high = [sb(f"high{s}", [P, DC, P], F32R) for s in range(RING)]
        low = [sb(f"low{s}", [P, DC, P], F32R) for s in range(RING)]
        mov_h = sb("mov_h", [P, DC, T], F32R)
        mov_l = sb("mov_l", [P, DC, T], F32R)
        sm = sb("sm", [P, SMALL], F32)
        mod = sb("mod", [P, MODS * DC], F32)
        gs = sb("gs", [P, DC], F32)
        cact = sb("cact", [P, DC], F32)
        ctmp = sb("ctmp", [P, DC], F32)
        ones = sb("ones", [P, P], F32)
        eps = sb("eps", [P, 1], F32)
        warm = sb("warm", [P, 1], F32)
        zeros = sb("zeros", [P, P], BF16)
        idx1 = sb("idx1", [P, T], BF16)
        idx2 = sb("idx2", [P, T], BF16)
        gate = sb("gate", [P, PARTS, T], BF16)
        hot1 = sb("hot1", [P, 2, PARTS, SET, HALF], BF16)
        hot2 = sb("hot2", [P, 2, SET, P], BF16)

        gate_rest = hot2[:].rearrange("p a b c -> p (a b c)").bitcast(F32)[:, 0:T]
        iota = sm[:, C_IOTA:C_IOTA + P]
        eye = sm[:, C_EYE:C_EYE + P]

        def part(a, n):
            return A[:, a:a + n]

        X = part(0, DC * T).rearrange("p (c t) -> p c t", c=DC)
        MT0 = DC * T
        mtile = part(MT0, 2 * D).rearrange("p (s n) -> p s n", s=2)
        MA0 = MT0 + 2 * D
        macc = part(MA0, MODS * D).rearrange("p (m n) -> p m n", m=MODS)
        N0 = MA0 + MODS * D
        ntile = part(N0, NEXT * D).rearrange("p (s n) -> p s n", s=NEXT)
        sd = part(N0, TC)
        rstd = part(N0 + TC, TC)
        diag = part(N0 + 2 * TC, T).rearrange("p (c t) -> p c t", c=TC)
        total = part(N0 + 3 * T, T)
        SQ0 = N0 + D
        sq = part(SQ0, DC * T).rearrange("p (c t) -> p c t", c=DC)
        XR0 = SQ0 + DC * T
        xr = part(XR0, DC * T).rearrange("p (c t) -> p c t", c=DC)
        keys = part(XR0 + DC * T, 2 * P).rearrange("p (s n) -> p s n", s=2)
        B0 = HALF * T
        mhead = part(B0, 2 * DC * D).rearrange("p (m k n) -> p m k n", m=2, k=DC)
        vp = part(B0, 2 * (T + 2)).rearrange("p (s t) -> p s t", s=2)
        cs = part(B0 + 1024, 2 * T).rearrange("p (s t) -> p s t", s=2)
        cv = part(B0 + 1536, 3 * T).rearrange("p (s t) -> p s t", s=3)
        Z0 = B0 + 2560
        Z = part(Z0, DC * T).rearrange("p (c t) -> p c t", c=DC)
        UP = part(B0 + 4864, DC * (PAD + T)).rearrange("p (c t) -> p c t", c=DC)
        W1 = part(B0 + 7168, 2 * (PAD + T)).rearrange("p (c t) -> p c t", c=2)
        W2 = part(B0 + 7936, 2 * (PAD + T)).rearrange("p (c t) -> p c t", c=2)
        WS = part(B0 + 8704, 2 * PAD).rearrange("p (c t) -> p c t", c=2)
        ROWS = TC * HEADS
        S0 = B0
        S = part(S0, ROWS * 2 * KEYS)
        Q0 = S0 + ROWS * 2 * KEYS
        Q = part(Q0, 2 * HEADS * T).rearrange("p (n t) -> p n t", n=2 * HEADS)
        EQ = part(Q0, T * TOPK)
        o = B0 + 12288
        SC = part(o, T)
        FL = part(o + 256, T).bitcast(U32)
        IDX = part(o + 512, 2 * T)
        ABu = part(o + 1024, 2 * T).bitcast(U32)
        AB = part(o + 1536, 2 * T)
        EX = part(o + 2048, 2 * T)
        GT = part(o + 2560, T)
        SUM = part(o + 2816, ROWS)
        RS = part(o + 2832, ROWS)
        s2 = part(o + 2848, 2 * KEYS).rearrange("p (s n) -> p s n", s=2)
        s3 = part(o + 3104, 2 * KEYS).rearrange("p (s n) -> p s n", s=2)
        v16 = part(o + 3360, 2 * TOPK).rearrange("p (s n) -> p s n", s=2)
        i16 = part(o + 3392, 2 * TOPK).rearrange("p (s n) -> p s n", s=2).bitcast(U32)
        cand = part(o + 3424, TOPK * TOPK)
        cand2 = part(o + 3680, TOPK * TOPK)
        b16 = part(o + 3936, TOPK)
        f16 = part(o + 3952, TOPK).bitcast(U32)

        def psum(name, n):
            return ctx.enter_context(nc.psum_tensor(name, [P, n, 512], F32))

        ps = psum("ps", 2)
        gp = psum("gp", 2)
        acc = psum("acc", 4)

        raw_full = [sem(f"raw_full{s}") for s in range(RING)]
        high_ready = sem("high_ready")
        low_ready = sem("low_ready")
        product = sem("product")
        evac_dve = sem("evac_dve")
        evac_act = sem("evac_act")
        small_in, x_in_s, keys_in = sem("small_in"), sem("x_in_s"), sem("keys_in")
        mhead_in = [sem(f"mhead_in{n}") for n in range(len(HEAD))]
        mtile_in = [sem(f"mtile_in{n}") for n in range(2)]
        shift2_in = [sem(f"shift2_in{n}") for n in range(2)]
        shift2_used = sem("shift2_used")
        mtile_used = sem("mtile_used")
        next_in = [sem(f"next_in{n}") for n in range(NEXT)]
        next_used = sem("next_used")
        macc_done = sem("macc_done")
        msum_done = sem("msum_done")
        mod_taken = sem("mod_taken")
        const_ready = sem("const_ready")
        cexp = sem("cexp")
        x_ready = sem("x_ready")
        warmed = sem("warmed")
        sq_done, stat_done, sd_done = sem("sq_done"), sem("stat_done"), sem("sd_done")
        diag_done, spread_done = sem("diag_done"), sem("spread_done")
        total_done = sem("total_done")
        xr_done, mh_done, ml_done = sem("xr_done"), sem("mh_done"), sem("ml_done")
        z_ready = sem("z_ready")
        score_done, score_out = sem("score_done"), sem("score_out")
        soft_in, soft_exp = sem("soft_in"), sem("soft_exp")
        pick_done = sem("pick_done")
        turned, turned_out = sem("turned"), sem("turned_out")
        hot_eq = sem("hot_eq")
        hot1_ready = sem("hot1_ready")
        scattered, weighted = sem("scattered"), sem("weighted")
        wh_ready, wl_ready = sem("wh_ready"), sem("wl_ready")
        spilled, reloaded = sem("spilled"), sem("reloaded")
        acc_done = sem("acc_done")
        step = sem("step")
        stored = sem("stored")

        def flat(t):
            return t[:].rearrange("p a b -> p (a b)")

        block = ctx.enter_context(nc.Block())

        @block.sync
        def _(sp):
            sp.sem_inc(mtile_used, 2)
            sp.sem_inc(next_used, NEXT)
            sp.dma_start(sm[:], small).then_inc(small_in, 16)

            def load(layer, name, j, s):
                n0 = AT[layer, name]
                static = isinstance(j, int)
                if not (static and n0 + j < RING):
                    sp.wait_ge(low_ready, j + (n0 - RING + 1))
                src = tiles_of[name, layer]
                src = src[j] if static else src[bass.ds(j, 1)].rearrange("a p n -> (a p) n")
                sp.dma_start(raw[:, s], src).then_inc(raw_full[s], 16)

            def load_mod(layer, m, k, t, slot):
                sp.wait_ge(mtile_used, t + 1)
                sp.dma_start(mtile[:, slot], w_mod[layer, k * P:(k + 1) * P, m * D:(m + 1) * D]
                             ).then_inc(mtile_in[slot], 16)

            for n, (m, k, ks) in enumerate(HEAD):
                if n == 2:
                    sp.dma_start(A[:, 0:DC * T], x_in).then_inc(x_in_s, 16)
                if n == len(HEAD) - 2:
                    load(0, "conv_in", 0, 0)
                sp.dma_start(mhead[:, m, k:k + ks],
                             w_mod[0, k * P:(k + ks) * P, m * D:(m + 1) * D].rearrange("(k p) n -> p k n", p=P)
                             ).then_inc(mhead_in[n], 16)

            mods = [(m, k) for k in range(DC) for m in (2, 4)]
            behind = [3 + 3 * (u // 2) + 2 * (u % 2) for u in range(2 * DC)]
            shift2 = {10: 0, 18: 1, 24: 2, 25: 3, 27: 4, 28: 5, 30: 6, 31: 7}
            for t in range(1, 32):
                if t < 24:
                    load(0, "conv_in", t, t % RING)
                elif t < 32:
                    load(0, "conv_out", t - 24, t % RING)
                for u in range(2 * DC):
                    if behind[u] == t:
                        load_mod(0, *mods[u], u, u % 2)
                if t in shift2:
                    n = shift2[t]
                    sp.wait_ge(macc_done, 1)
                    if n >= 2:
                        sp.wait_ge(shift2_in[n % 2], (n // 2) * 16)
                    sp.dma_start(mhead[:, 1, n], w_mod[0, n * P:(n + 1) * P, 3 * D:4 * D]
                                 ).then_inc(shift2_in[n % 2], 16)

            def run(layer, name, tiles, first=0):
                with sp.Fori(0, tiles // RING) as i:
                    for s in range(RING):
                        load(layer, name, i * RING + (first + s), s)

            for layer in range(LAYERS):
                if layer == 1:
                    run(1, "pool_in", 8)
                    run(1, "pool_group", 4)
                    run(1, "pool_out", 8)
                with sp.Fori(0, 16 // RING) as i:
                    for s in range(RING):
                        load(layer, "query", i * RING + s, s)
                        if s % 2:
                            sp.wait_ge(mtile_used, i * 2 + ((2 + layer) * DC + s // 2 + 1))
                            w = w_mod[layer, :, 5 * D:6 * D].rearrange("(k p) n -> k p n", p=P)
                            sp.dma_start(mtile[:, s // 2], w[bass.ds(i * 2 + s // 2, 1)].rearrange("a p n -> (a p) n")
                                         ).then_inc(mtile_in[s // 2], 16)
                run(layer, "up", KEYS)
                run(layer, "down", HALF)
                for q in range(RING):
                    load(layer, "down", HALF + q, q)
                sp.wait_ge(wl_ready, (2 * layer + 1) * HALF)
                sp.wait_ge(spilled, 16 * (layer + 1))
                sp.dma_start(A[:, 0:DC * T], x_spill).then_inc(reloaded, 16)
                if layer == 1:
                    run(1, "down", HALF - RING, HALF + RING)
                else:
                    sp.dma_start(keys, k_t[1]).then_inc(keys_in, 16)

                    def next_mod(i, q):
                        sp.wait_ge(next_used, i * NEXT + (q + 1))
                        w = w_mod[1, :, q * D:(q + 1) * D].rearrange("(k p) n -> k p n", p=P)
                        sp.dma_start(ntile[:, q], w[bass.ds(i, 1)].rearrange("a p n -> (a p) n")
                                     ).then_inc(next_in[q], 16)

                    for q in range(8):
                        if q >= RING:
                            load(0, "down", HALF + q, q % RING)
                        if q < NEXT:
                            sp.wait_ge(next_used, q + 1)
                            sp.dma_start(ntile[:, q], w_mod[1, 0:P, q * D:(q + 1) * D]).then_inc(next_in[q], 16)
                    with sp.Fori(0, DC - 1) as i:
                        for q in range(8):
                            load(0, "down", i * 8 + (HALF + 8 + q), q % RING)
                            if q < NEXT:
                                next_mod(i + 1, q)
            for n in range(4):
                sp.wait_ge(xr_done, 4 * DC + 2 * n + 2)
                sp.dma_start(out[:, 2 * n * T:(2 * n + 2) * T],
                             A[:, B0 + 2 * n * T:B0 + (2 * n + 2) * T]).then_inc(stored, 16)
            sp.wait_ge(stored, 4 * 16)

        @block.gpsimd
        def _(pool):
            nc.gpsimd.memset(ones[:], 1.0).then_inc(const_ready, 1)
            nc.gpsimd.memset(eps[:], EPS).then_inc(const_ready, 1)
            nc.gpsimd.memset(zeros[:], 0.0).then_inc(const_ready, 1)
            nc.gpsimd.memset(macc[:, 2:MODS].rearrange("p m n -> p (m n)"), 0.0).then_inc(const_ready, 1)
            with pool.Fori(0, TILES // RING) as i:
                for s in range(RING):
                    pool.wait_ge(high_ready, i * RING + (s + 1))
                    nc.gpsimd.tensor_tensor(flat(low[s]), raw[:, s], flat(high[s]).bitcast(F32),
                                            ALU.subtract).then_inc(low_ready, 1)

        @block.scalar
        def _(act):
            act.sem_inc(evac_act, 2)
            act.sem_inc(evac_dve, 2)

            def round_tile(n, s):
                act.wait_ge(product, n + 1)
                nc.scalar.activation(flat(high[s]), raw[:, s], ACT.Copy).then_inc(high_ready, 1)

            def arrived(k, s):
                act.wait_ge(raw_full[s], k * 16)

            def ahead(i, n0, s):
                t = s + AHEAD
                arrived(i + (n0 // RING + t // RING + 1), t % RING)
                round_tile(i * RING + (n0 + t), t % RING)

            def load_table(n):
                nc.scalar.activation(warm[:], eps[:], ACT.Sqrt).then_inc(warmed, 1)
                act.wait_ge(warmed, n)

            def norm(k):
                if k % 2 == 0:
                    for c in range(DC):
                        if k == 0:
                            act.wait_ge(x_in_s, 16)
                        else:
                            act.wait_ge(x_ready, (k // 2 - 1) * DC + c + 1)
                        nc.scalar.activation(sq[:, c], X[:, c], ACT.Square).then_inc(sq_done, 1)
                else:
                    act.dma_start(x_spill, flat2(X)).then_inc(spilled, 16)
                act.wait_ge(stat_done, k + 1)
                nc.scalar.activation(sd, gp[:, 0, 0:TC], ACT.Sqrt, bias=eps[:, 0:1],
                                     scale=1.0 / D).then_inc(sd_done, 1)
                if k == 4:
                    return
                if k == 0:
                    for n in range(AHEAD):
                        arrived(1, n)
                        nc.scalar.activation(flat(high[n]), raw[:, n], ACT.Copy).then_inc(high_ready, 1)
                shift = mod[:, (3 * (k % 2)) * DC:(3 * (k % 2) + 1) * DC]
                act.wait_ge(mod_taken, (2, 4, 6, 7)[k])
                for c in range(DC):
                    act.wait_ge(xr_done, DC * k + c + 1)
                    nc.scalar.activation(mov_h[:, c], xr[:, c], ACT.Identity,
                                         bias=shift[:, c:c + 1]).then_inc(mh_done, 1)

            def flat2(v):
                return v.rearrange("p c t -> p (c t)")

            def split_z(n_products, ready):
                act.wait_ge(product, n_products + RING)
                for c in range(DC):
                    act.wait_ge(*ready(c))
                    nc.scalar.activation(mov_h[:, c], Z[:, c], ACT.Copy).then_inc(mh_done, 1)

            def only_round(n0, tiles):
                with act.Fori(0, tiles // RING) as i:
                    for s in range(RING):
                        ahead(i, n0, s)

            def round_and_square(n0, evac0):
                with act.Fori(0, DC // RING) as i:
                    for s in range(RING):
                        ahead(i, n0, s)
                        act.wait_ge(evac_dve, i * RING + (2 + evac0 + s + 1))
                        nc.scalar.activation(A[:, bass.ds(i * (RING * T) + (SQ0 + s * T), T)],
                                             A[:, bass.ds(i * (RING * T) + s * T, T)], ACT.Square
                                             ).then_inc(sq_done, 1)

            act.dma_start(keys, k_t[0]).then_inc(keys_in, 16)
            act.wait_ge(small_in, 16)
            nc.scalar.activation(ctmp[:], sm[:, C_C:C_C + DC], ACT.Exp, scale=-1.0).then_inc(cexp, 1)
            act.wait_ge(const_ready, 2)
            load_table(1)
            for layer in range(LAYERS):
                norm_k = 2 * layer
                norm(norm_k)
                if layer == 0:
                    only_round(AT[0, "conv_in"], 24)
                    split_z(AT[0, "conv_out"], lambda c: (evac_dve, 2 + 3 * (c + 1)))
                    round_and_square(AT[0, "conv_out"], 24)
                else:
                    only_round(AT[1, "pool_in"], 8)
                    split_z(AT[1, "pool_group"], lambda c: (z_ready, c + 1))
                    only_round(AT[1, "pool_group"], 4)
                    split_z(AT[1, "pool_out"], lambda c: (evac_dve, 2 + 32 + 8 + c // 2 + 1))
                    round_and_square(AT[1, "pool_out"], 44)
                norm(norm_k + 1)
                n0 = AT[layer, "query"]
                with act.Fori(0, 16 // RING) as i:
                    for s in range(RING):
                        ahead(i, n0, s)
                        act.wait_ge(product, i * RING + (n0 + s + 1 + RING))
                        nc.scalar.activation(A[:, bass.ds(i * (RING * T) + (Q0 + s * T), T)],
                                             ps[:, s % 2, 0:T], ACT.Copy).then_inc(evac_act, 1)
                act.wait_ge(spilled, 16 * (layer + 1))
                n0 = AT[layer, "up"]

                def gelus(first, trips):
                    with act.Fori(0, trips) as i:
                        for s in range(RING):
                            ahead(i, n0 + first, s)
                            act.wait_ge(product, i * RING + (n0 + first + s + 1 + RING))
                            nc.scalar.activation(A[:, bass.ds(i * (RING * T) + (first + s) * T, T)],
                                                 ps[:, s % 2, 0:T], ACT.Gelu).then_inc(evac_act, 1)

                gelus(0, HALF // RING - 4)
                act.wait_ge(soft_in, layer + 1)
                nc.scalar.activation(SC, SC, ACT.Exp).then_inc(soft_exp, 1)
                gelus(HALF - 4 * RING, 4)
                act.wait_ge(turned, layer + 1)
                gelus(HALF, HALF // RING)

                n0 = AT[layer, "down"]

                def weight(g, s):
                    nc.scalar.activation(mov_h[:, s], A[:, bass.ds(g * T, T)] if not isinstance(g, int)
                                         else A[:, g * T:(g + 1) * T], ACT.Copy).then_inc(wh_ready, 1)

                for half in range(2):
                    first = half * HALF
                    act.wait_ge(weighted, (2 * layer + half + 1) * SETS)
                    for s in range(AHEAD):
                        act.wait_ge(product, n0 + first + s + 1 + (RING - 1 - s if half == 0 else 0))
                        weight(first + s, s)
                    with act.Fori(0, HALF // RING - 1) as i:
                        for s in range(RING):
                            ahead(i, n0 + first, s)
                            weight(i * RING + (first + s + AHEAD), (s + AHEAD) % RING)
                    last = n0 + first + HALF - RING
                    if half == 1:
                        load_table(layer + 2)
                    for s in range(RING):
                        if last + s + AHEAD < TILES:
                            ahead(0, last, s)
                        if s + AHEAD < RING:
                            if last + s + AHEAD >= TILES:
                                act.wait_ge(product, last + s + AHEAD + 1)
                            weight(first + HALF - RING + s + AHEAD, (s + AHEAD) % RING)
            norm(4)

        @block.vector
        def _(dve):
            link = Chain(dve, step)

            def turn(v, n):
                return v.rearrange("p (r n) -> p r n", n=n)

            dve.wait_ge(cexp, 1)
            link(nc.vector.tensor_scalar(ctmp[:], ctmp[:], 1.0, None, ALU.add))
            link(nc.vector.reciprocal(ctmp[:], ctmp[:]))
            link(nc.vector.tensor_tensor(cact[:], ctmp[:], sm[:, C_C:C_C + DC], ALU.mult))

            def add_mod(m, tile, k, first):
                c = cact[:, k:k + 1] if isinstance(k, int) else cact[:, bass.ds(k, 1)]
                if first:
                    return nc.vector.tensor_scalar(macc[:, m], tile, c, None, ALU.mult)
                return nc.vector.scalar_tensor_tensor(macc[:, m], tile, c, macc[:, m], ALU.mult, ALU.add)

            def head_mod(m):
                for n, (block_, k0, ks) in enumerate(HEAD):
                    if block_ == m:
                        dve.wait_ge(mhead_in[n], 16)
                        for k in range(k0, k0 + ks):
                            link(add_mod(m, mhead[:, m, k], k, k == 0))
                dve.sem_inc(macc_done, 1)

            sums = [0]

            def finish_mod(layer, ms):
                sums[0] += 1
                dve.wait_ge(msum_done, sums[0])
                for m in ms:
                    a, b = m * DC, (m + 1) * DC
                    bm = C_BM + layer * MODS * DC
                    ins = nc.vector.tensor_tensor(mod[:, a:b], gp[:, 1, a:b], sm[:, bm + a:bm + b], ALU.add)
                ins.then_inc(mod_taken, 1)
                dve.wait_ge(mod_taken, sums[0])

            def norm(k, shift_last=None):
                g0 = (C_N1, C_N2)[k % 2] + (k // 2) * DC
                if k == 0:
                    head_mod(1)
                dve.wait_ge(sd_done, k + 1)
                link(nc.vector.reciprocal(rstd, sd))
                for tc in range(TC):
                    nc.vector.tensor_scalar(diag[:, tc], eye, rstd[:, tc:tc + 1], None, ALU.mult
                                            ).then_inc(diag_done, 1)
                if k == 0:
                    head_mod(0)
                    finish_mod(0, (1,))
                if k < 4:
                    scale = mod[:, (3 * (k % 2) + 1) * DC:(3 * (k % 2) + 2) * DC]
                    link(nc.vector.scalar_tensor_tensor(gs[:], scale, 1.0, sm[:, g0:g0 + DC], ALU.add, ALU.mult))
                    weight = gs[:]
                else:
                    weight = sm[:, C_FG:C_FG + DC]
                dve.wait_ge(spread_done, k + 1)
                if k < 4:
                    shift = mod[:, (3 * (k % 2)) * DC:(3 * (k % 2) + 1) * DC]

                def scaled(c):
                    dst = xr[:, c] if k < 4 else A[:, B0 + c * T:B0 + (c + 1) * T]
                    nc.vector.scalar_tensor_tensor(dst, X[:, c], weight[:, c:c + 1], gp[:, 0, T:2 * T], ALU.mult,
                                                   ALU.mult).then_inc(xr_done, 1)

                def rest(c):
                    moved[0] += 1
                    dve.wait_ge(mh_done, moved[0])
                    nc.vector.scalar_tensor_tensor(mov_l[:, c], xr[:, c], shift[:, c:c + 1],
                                                   mov_h[:, c].bitcast(F32), ALU.add,
                                                   ALU.subtract).then_inc(ml_done, 1)

                lag = 4 if shift_last else 2
                for c in range(DC):
                    if shift_last and c == lag:
                        shift_last()
                    scaled(c)
                    if k < 4 and c >= lag:
                        rest(c - lag)
                if k < 4:
                    for c in range(DC - lag, DC):
                        rest(c)

            moved = [0]

            def split_z():
                for c in range(DC):
                    moved[0] += 1
                    dve.wait_ge(mh_done, moved[0])
                    nc.vector.tensor_tensor(mov_l[:, c], Z[:, c], mov_h[:, c].bitcast(F32),
                                            ALU.subtract).then_inc(ml_done, 1)

            def bank(n0, j, s):
                dve.wait_ge(product, j + (n0 + 1 + RING))
                return ps[:, s % 2, 0:T]

            def use_mtile(m, k, t, slot):
                dve.wait_ge(mtile_in[slot], t)
                add_mod(m, mtile[:, slot], k, False).then_inc(mtile_used, 1)

            def residual(n0, layer):
                t0 = layer * (DC - 1)

                def add_squares(c):
                    if c >= 2:
                        dve.wait_ge(total_done, t0 + c - 1)
                    dve.wait_ge(sq_done, (2 * layer + 1) * DC + c + 1)
                    nc.vector.tensor_tensor(total, sq[:, 0] if c == 1 else total, sq[:, c],
                                            ALU.add).then_inc(total_done, 1)

                for c in range(DC):
                    if layer == 0:
                        dve.wait_ge(shift2_in[c % 2], (c // 2 + 1) * 16)
                        if c:
                            dve.wait_ge(shift2_used, c)
                        add_mod(3, mhead[:, 1, c], c, c == 0).then_inc(shift2_used, 1)
                    if c >= 2:
                        add_squares(c - 1)
                    dve.wait_ge(product, n0 + c + 1 + RING)
                    nc.vector.scalar_tensor_tensor(X[:, c], ps[:, c % 2, 0:T], mod[:, 2 * DC + c:2 * DC + c + 1],
                                                   X[:, c], ALU.mult, ALU.add).then_inc(evac_dve, 1)
                add_squares(DC - 1)

            def picks(rows):
                met = (score_out, 1)
                for src, spare, vals, idx in rows:
                    ins = nc.vector.max(vals[:, 0:8], src)
                link(ins, met=met)
                for src, spare, vals, idx in rows:
                    nc.vector.max_index(idx[:, 0:8], vals[:, 0:8], src)
                    ins = nc.vector.match_replace(spare, vals[:, 0:8], src, LOWEST)
                link(ins, met=met)
                for src, spare, vals, idx in rows:
                    ins = nc.vector.max(vals[:, 8:16], spare)
                link(ins, met=met)
                for src, spare, vals, idx in rows:
                    ins = nc.vector.max_index(idx[:, 8:16], vals[:, 8:16], spare)
                return ins

            for layer in range(LAYERS):
                if layer == 0:
                    norm(0, lambda: finish_mod(0, (0,)))
                    n0 = AT[0, "conv_in"]
                    link(nc.vector.memset(vp, 0.0))
                    dve.wait_ge(const_ready, 4)
                    with dve.Fori(0, 4) as i:
                        link.enter(i, 6)
                        for q in range(2):
                            s = 3 * q
                            w = [sm[:, bass.ds(i * 2 + (C_CW + k * DC + q), 1)] for k in range(TAPS)]
                            z = A[:, bass.ds(i * (2 * T) + (Z0 + q * T), T)]
                            p = bank(n0, i * 6 + s, s)
                            nc.vector.tensor_copy(cs[:, q], p).then_inc(evac_dve, 1)
                            use_mtile(2, i * 2 + q, i * (2 * 16) + (q + 1) * 16, 0)
                            p = bank(n0, i * 6 + s + 1, s + 1)
                            dve.wait_ge(evac_dve, i * 6 + (2 + s + 1))
                            nc.vector.tensor_tensor(vp[:, q, 2:2 + T], p, cs[:, q], ALU.mult).then_inc(evac_dve, 1)
                            dve.wait_ge(evac_dve, i * 6 + (2 + s + 2))
                            link(nc.vector.tensor_scalar(cv[:, 0], vp[:, q, 0:T], w[0], None, ALU.mult))
                            link(nc.vector.scalar_tensor_tensor(cv[:, 1], vp[:, q, 1:1 + T], w[1], cv[:, 0],
                                                                ALU.mult, ALU.add))
                            link(nc.vector.scalar_tensor_tensor(cv[:, 2], vp[:, q, 2:2 + T], w[2], cv[:, 1],
                                                                ALU.mult, ALU.add))
                            p = bank(n0, i * 6 + s + 2, s + 2)
                            nc.vector.tensor_tensor(z, p, cv[:, 2], ALU.mult).then_inc(evac_dve, 1)
                            use_mtile(4, i * 2 + q, i * (2 * 16) + (q + 1) * 16, 1)
                            dve.wait_ge(mtile_used, i * 4 + (2 + 2 * q + 2))
                        link.leave(4)
                    split_z()
                    finish_mod(0, (2,))
                    residual(AT[0, "conv_out"], 0)
                    finish_mod(0, (3, 4))
                    norm(1)
                else:
                    dve.wait_ge(x_ready, DC)
                    finish_mod(1, (0, 1))
                    norm(2)
                    n0 = AT[1, "pool_in"]
                    link(nc.vector.memset(UP[:, :, 0:PAD], 0.0))
                    for g, w in enumerate(WINDOWS):
                        for j in (2 * g, 2 * g + 1):
                            p = bank(n0, j, j)
                            nc.vector.tensor_copy(UP[:, j, PAD:PAD + T], p).then_inc(evac_dve, 1)
                        dve.wait_ge(evac_dve, 2 + 32 + 2 * g + 2)
                        src, span, spare = UP[:, 2 * g:2 * g + 2], 1, [W1, W2]
                        end = PAD + T
                        while span < w:
                            dst = spare[0]
                            lo = 2 * span - 1
                            link(nc.vector.tensor_tensor(dst[:, :, lo:end], src[:, :, lo:end],
                                                         src[:, :, lo - span:end - span], ALU.add))
                            src, span, spare = dst, 2 * span, spare[::-1]
                        u = UP[:, 2 * g:2 * g + 2]
                        z = Z[:, 2 * g:2 * g + 2]
                        counts = sm[:, C_CNT + g * PAD:C_CNT + (g + 1) * PAD].unsqueeze(1).broadcast_to([P, 2, PAD])
                        link(nc.vector.tensor_tensor(WS, src[:, :, PAD:2 * PAD], counts, ALU.mult))
                        link(nc.vector.scalar_tensor_tensor(z, src[:, :, PAD:end], 1.0 / w, u[:, :, PAD:end],
                                                            ALU.mult, ALU.subtract))
                        nc.vector.tensor_tensor(z[:, :, 0:PAD], WS, u[:, :, PAD:2 * PAD],
                                                ALU.subtract).then_inc(z_ready, 2)
                    split_z()
                    finish_mod(1, (2, 3))
                    n0 = AT[1, "pool_group"]
                    for j in range(4):
                        dve.wait_ge(product, n0 + j + 1 + RING)
                        for c in range(2):
                            scale = sm[:, C_PS + 2 * j + c:C_PS + 2 * j + c + 1]
                            ins = nc.vector.tensor_scalar(Z[:, 2 * j + c], ps[:, j % 2, c * T:(c + 1) * T], scale,
                                                          None, ALU.mult)
                        ins.then_inc(evac_dve, 1)
                    split_z()
                    finish_mod(1, (4,))
                    residual(AT[1, "pool_out"], 1)
                    norm(3)
                for k in range(DC):
                    t = (2 + layer) * DC + k
                    dve.wait_ge(mtile_in[k % 2], (t // 2 + 1) * 16)
                    add_mod(5, mtile[:, k % 2], k, k == 0).then_inc(mtile_used, 1)
                    dve.wait_ge(mtile_used, 2 + t + 1)
                finish_mod(layer, (5,))

                for n in range(8):
                    dve.wait_ge(score_done, 8 * layer + n + 1)
                    nc.vector.tensor_copy(S[:, n * 512:(n + 1) * 512], gp[:, n % 2, :]).then_inc(score_out, 1)
                dve.wait_ge(score_out, 8 * (layer + 1))
                with dve.Fori(0, ROWS) as i:
                    link.enter(i, 10)
                    link(nc.vector.tensor_copy(s2.rearrange("p s n -> p (s n)"),
                                               A[:, bass.ds(i * (2 * KEYS) + B0, 2 * KEYS)]), met=(score_out, 1))
                    picks([(s2[:, side], s3[:, side], v16[:, side], i16[:, side]) for side in range(2)])
                    link(nc.vector.tensor_tensor(cand.rearrange("p (a b) -> p a b", a=TOPK),
                                                 v16[:, 0].unsqueeze(2).broadcast_to([P, TOPK, TOPK]),
                                                 v16[:, 1].unsqueeze(1).broadcast_to([P, TOPK, TOPK]), ALU.add),
                         met=(score_out, 1))
                    link(picks([(cand, cand2, b16, f16)]))
                    nc.vector.tensor_copy(A[:, bass.ds(i * TOPK + o, TOPK)], b16)
                    nc.vector.tensor_copy(A[:, bass.ds(i * TOPK + (o + 256), TOPK)].bitcast(U32), f16)
                    link(nc.vector.tensor_copy(A[:, bass.ds(i * (2 * TOPK) + (o + 512), 2 * TOPK)],
                                               i16.rearrange("p s n -> p (s n)")))
                    link.leave(ROWS)
                sc3 = turn(SC, TOPK)
                link(nc.vector.tensor_copy(RS, sc3[:, :, 0]))
                nc.vector.tensor_tensor(sc3, sc3, RS.unsqueeze(2).broadcast_to([P, ROWS, TOPK]),
                                        ALU.subtract).then_inc(soft_in, 1)
                nc.vector.tensor_scalar(ABu[:, 0:T], FL, 4, None, ALU.logical_shift_right)
                link(nc.vector.tensor_scalar(ABu[:, T:2 * T], FL, TOPK - 1, None, ALU.bitwise_and))
                link(nc.vector.tensor_copy(AB, ABu))
                idx4 = IDX.rearrange("p (r s n) -> p r s n", s=2, n=TOPK)
                for side in range(2):
                    eq = EQ.rearrange("p (r k) -> p r k", k=TOPK)
                    link(nc.vector.tensor_tensor(eq, AB[:, side * T:(side + 1) * T].unsqueeze(2)
                                                 .broadcast_to([P, T, TOPK]),
                                                 iota[:, 0:TOPK].unsqueeze(1).broadcast_to([P, T, TOPK]),
                                                 ALU.is_equal))
                    eq4 = EQ.rearrange("p (r k n) -> p r k n", k=TOPK, n=TOPK)
                    link(nc.vector.tensor_tensor(eq4, eq4, idx4[:, :, side].unsqueeze(2)
                                                 .broadcast_to([P, ROWS, TOPK, TOPK]), ALU.mult))
                    link(nc.vector.tensor_reduce(EX[:, side * T:(side + 1) * T], eq, AX_X, ALU.add))
                dve.wait_ge(soft_exp, layer + 1)
                link(nc.vector.tensor_reduce(SUM, sc3, AX_X, ALU.add))
                link(nc.vector.reciprocal(RS, SUM))
                nc.vector.tensor_tensor(turn(GT, TOPK), sc3, RS.unsqueeze(2).broadcast_to([P, ROWS, TOPK]),
                                        ALU.mult).then_inc(pick_done, 1)
                dve.wait_ge(turned, layer + 1)
                nc.vector.tensor_copy(idx1[:], gp[:, 0, 0:T]).then_inc(turned_out, 1)
                nc.vector.tensor_copy(idx2[:], gp[:, 0, T:2 * T]).then_inc(turned_out, 1)
                link(nc.vector.tensor_copy(gate[:, 0], gp[:, 1, 0:T]))
                nc.vector.tensor_tensor(gate_rest, gp[:, 1, 0:T], gate[:, 0], ALU.subtract).then_inc(turned_out, 1)
                dve.wait_ge(turned_out, 3 * (layer + 1))
                link(nc.vector.tensor_copy(gate[:, 1], gate_rest))
                link(nc.vector.tensor_tensor(gate_rest, gate_rest, gate[:, 1], ALU.subtract))
                link(nc.vector.tensor_copy(gate[:, 2], gate_rest))

                def hots(half, i, u):
                    def over(v, n):
                        v = v[:, bass.ds(i * (2 * SET) + u * SET, SET)]
                        return v.unsqueeze(2).broadcast_to([P, SET, n])

                    def number(a, b):
                        return iota[:, a:b].unsqueeze(1).broadcast_to([P, SET, b - a])

                    k0 = (2 * layer + half) * SETS
                    eq = hot1[:, u, PARTS - 1]
                    nc.vector.tensor_tensor(eq, number(half * HALF, (half + 1) * HALF), over(idx1, HALF),
                                            ALU.is_equal).then_inc(hot_eq, 1)
                    dve.wait_ge(hot_eq, i * 4 + (2 * (k0 + u) + 1))
                    g = gate[:, 0:PARTS - 1, bass.ds(i * (2 * SET) + u * SET, SET)]
                    nc.vector.tensor_tensor(hot1[:, u, 0:PARTS - 1],
                                            eq.unsqueeze(1).broadcast_to([P, PARTS - 1, SET, HALF]),
                                            g.unsqueeze(3).broadcast_to([P, PARTS - 1, SET, HALF]), ALU.mult
                                            ).then_inc(hot_eq, 1)
                    nc.vector.tensor_tensor(hot2[:, u], number(0, P), over(idx2, P), ALU.is_equal)
                    dve.wait_ge(hot_eq, i * 4 + (2 * (k0 + u) + 2))
                    nc.vector.tensor_tensor(eq, eq, over(gate[:, PARTS - 1], HALF), ALU.mult
                                            ).then_inc(hot1_ready, 1)

                def weigh(half, i, u):
                    k0 = (2 * layer + half) * SETS
                    dve.wait_ge(scattered, i * 2 + (k0 + u + 1))
                    a = A[:, half * B0:half * B0 + HALF * T].rearrange("p (g t) -> p g t", t=T)
                    a = a[:, :, bass.ds(i * (2 * SET) + u * SET, SET)]
                    g = gp[:, u, :].rearrange("p (t g) -> p g t", t=SET)
                    nc.vector.tensor_tensor(a, a, g, ALU.mult).then_inc(weighted, 1)

                dve.wait_ge(evac_act, 2 + layer * (16 + KEYS) + 16 + HALF)
                hots(0, 0, 0)
                with dve.Fori(0, SETS // 2 - 1) as i:
                    for u in range(2):
                        hots(0, i + u, 1 - u)
                        weigh(0, i, u)
                hots(0, SETS // 2 - 1, 1)
                for u in range(2):
                    weigh(0, SETS // 2 - 1, u)

                n0 = AT[layer, "down"]

                def low_weight(g, s):
                    dve.wait_ge(wh_ready, g + (layer * KEYS + 1))
                    a = A[:, g * T:(g + 1) * T] if isinstance(g, int) else A[:, bass.ds(g * T, T)]
                    nc.vector.tensor_tensor(mov_l[:, s], a, mov_h[:, s].bitcast(F32),
                                            ALU.subtract).then_inc(wl_ready, 1)

                for s in range(AHEAD):
                    low_weight(s, s)
                hots(1, 0, 0)
                dve.wait_ge(evac_act, 2 + (layer + 1) * (16 + KEYS))
                with dve.Fori(0, HALF // RING - 1) as i:
                    for s in range(RING):
                        if s % 2 == 0:
                            hots(1, i + s // 2, 1 - s // 2)
                        low_weight(i * RING + (s + AHEAD), (s + AHEAD) % RING)
                        if s % 2:
                            weigh(1, i, s // 2)
                last = HALF - RING
                hots(1, SETS // 2 - 1, 1)
                low_weight(last + AHEAD, AHEAD)
                for u in range(2):
                    weigh(1, SETS // 2 - 1, u)
                for s in range(AHEAD):
                    low_weight(HALF + s, s)
                body = 8 if layer == 0 else RING

                def second(i, s, cut):
                    n = s + AHEAD
                    if not (cut and n >= body):
                        low_weight(i * body + (HALF + n), n % RING)
                    if layer == 0 and s < NEXT:
                        dve.wait_ge(next_in[s], i * 16 + 16)
                        first = isinstance(i, int) and i == 0
                        if not first:
                            dve.wait_ge(next_used, i * NEXT + (s + 1))
                        add_mod(s, ntile[:, s], i, first).then_inc(next_used, 1)

                for s in range(body):
                    second(0, s, False)
                with dve.Fori(0, HALF // body - 2) as i:
                    for s in range(body):
                        second(i + 1, s, False)
                for s in range(body):
                    second(HALF // body - 1, s, True)
                dve.wait_ge(reloaded, 16 * (layer + 1))
                for c in range(DC):
                    if c % 2 == 0 and c < DC - 2:
                        dve.wait_ge(acc_done, 3 * layer + c // 2 + 1)
                    elif c % 2 == 0:
                        dve.wait_ge(product, n0 + KEYS + RING)
                    nc.vector.scalar_tensor_tensor(X[:, c], acc[:, c // 2, (c % 2) * T:(c % 2 + 1) * T],
                                                   mod[:, 5 * DC + c:5 * DC + c + 1], X[:, c],
                                                   ALU.mult, ALU.add).then_inc(x_ready, 1)
            norm(4)

        @block.tensor
        def _(pe):
            pe.sem_inc(product, RING)
            pe.wait_ge(const_ready, 3)

            sums = [0]

            def sum_mod(ms):
                if sums[0]:
                    pe.wait_ge(mod_taken, sums[0])
                sums[0] += 1
                for m in ms:
                    for c in range(DC):
                        ins = nc.tensor.matmul(gp[:, 1, m * DC + c:m * DC + c + 1], macc[:, m, c * P:(c + 1) * P],
                                               ones[:, 0:1], start=True, stop=True)
                ins.then_inc(msum_done, 1)

            def token_sums(k, parts):
                for n, (sem_, value, src) in enumerate(parts):
                    pe.wait_ge(sem_, value)
                    for tc in range(TC):
                        ins = nc.tensor.matmul(gp[:, 0, tc:tc + 1], src[:, tc * P:(tc + 1) * P], ones[:, 0:1],
                                               start=(n == 0 and tc == 0), stop=(n == len(parts) - 1),
                                               skip_group_check=True)
                ins.then_inc(stat_done, 1)

            def square_sums(k):
                if k % 2:
                    token_sums(k, [(total_done, (k // 2 + 1) * (DC - 1), total)])
                else:
                    token_sums(k, [(sq_done, DC * k + c + 1, sq[:, c]) for c in range(DC)])

            def spread(k):
                for tc in range(TC):
                    pe.wait_ge(diag_done, TC * k + tc + 1)
                    ins = nc.tensor.matmul(gp[:, 0, T + tc * P:T + (tc + 1) * P], ones[:], diag[:, tc],
                                           start=True, stop=True)
                ins.then_inc(spread_done, 1)

            moved = [0]

            def moving(c):
                pe.wait_ge(ml_done, moved[0] * DC + c + 1)

            def three(dst, s, c, mv, first, last, skip=False):
                for n, (w, m) in enumerate(((high, mov_h), (high, mov_l), (low, mov_h))):
                    ins = nc.tensor.matmul(dst, w[s][:, c], m[:, mv], start=(first and n == 0),
                                           stop=(last and n == 2), skip_group_check=skip)
                return ins

            def project(layer, name, i, s, evac, evac0):
                pe.wait_ge(low_ready, i * RING + (AT[layer, name] + s + 1))
                pe.wait_ge(evac, i * RING + (evac0 + s + 1))
                for c in range(DC):
                    if s == 0:
                        moving(c)
                    ins = three(ps[:, s % 2, 0:T], s, c, c, c == 0, c == DC - 1)
                ins.then_inc(product, 1)

            def run(layer, name, tiles, evac, evac0):
                with pe.Fori(0, tiles // RING) as i:
                    for s in range(RING):
                        project(layer, name, i, s, evac, evac0)
                if name != "query":
                    moved[0] += 1

            for layer in range(LAYERS):
                out_act = layer * (16 + KEYS)
                if layer == 1:
                    pe.wait_ge(weighted, 2 * SETS)
                square_sums(2 * layer)
                if layer == 0:
                    pe.wait_ge(macc_done, 1)
                    sum_mod((1,))
                spread(2 * layer)
                if layer == 0:
                    pe.wait_ge(macc_done, 2)
                    sum_mod((0,))
                if layer == 0:
                    run(0, "conv_in", 24, evac_dve, 0)
                    pe.wait_ge(mtile_used, 2 + 2 * DC)
                    sum_mod((2,))
                    run(0, "conv_out", 8, evac_dve, 24)
                    pe.wait_ge(shift2_used, DC)
                    sum_mod((3, 4))
                    square_sums(1)
                else:
                    pe.wait_ge(evac_act, 2 + out_act)
                    run(1, "pool_in", 8, evac_dve, 32)
                    sum_mod((2, 3))
                    for s in range(RING):
                        pe.wait_ge(low_ready, AT[1, "pool_group"] + s + 1)
                        pe.wait_ge(evac_dve, 40 + s + 1)
                        for oc in range(2):
                            for kc in range(2):
                                pe.wait_ge(ml_done, moved[0] * DC + 2 * s + kc + 1)
                                ins = three(ps[:, s % 2, oc * T:(oc + 1) * T], s, 2 * oc + kc, 2 * s + kc,
                                            kc == 0, kc == 1)
                        ins.then_inc(product, 1)
                    moved[0] += 1
                    sum_mod((4,))
                    run(1, "pool_out", 8, evac_dve, 44)
                    square_sums(3)
                spread(2 * layer + 1)
                run(layer, "query", 16, evac_act, out_act)
                pe.wait_ge(mtile_used, 2 + (3 + layer) * DC)
                sum_mod((5,))
                pe.wait_ge(evac_act, 2 + out_act + 16)
                pe.wait_ge(keys_in, 16 * (layer + 1))
                for n in range(8):
                    if n == 1:
                        pe.wait_ge(mod_taken, sums[0])
                    elif n >= 2:
                        pe.wait_ge(score_out, 8 * layer + n - 1)
                    for q in range(4):
                        tc, hs = n // 4, 4 * (n % 4) + q
                        ins = nc.tensor.matmul(gp[:, n % 2, q * P:(q + 1) * P], Q[:, hs, tc * P:(tc + 1) * P],
                                               keys[:, hs % 2], start=True, stop=True)
                    ins.then_inc(score_done, 1)

                n0 = AT[layer, "up"]

                def up_tile(first, i, s):
                    pe.wait_ge(low_ready, i * RING + (n0 + first + s + 1))
                    pe.wait_ge(evac_act, i * RING + (out_act + 16 + first + s + 1))
                    for c in range(DC):
                        ins = three(ps[:, s % 2, 0:T], s, c, c, c == 0, c == DC - 1)
                    ins.then_inc(product, 1)

                def scatter(half, i, u):
                    k0 = (2 * layer + half) * SETS
                    pe.wait_ge(hot1_ready, i * 2 + (k0 + u + 1))
                    for j in range(SET):
                        for n in range(PARTS):
                            ins = nc.tensor.matmul(gp[:, u, j * HALF:(j + 1) * HALF], hot2[:, u, j],
                                                   hot1[:, u, n, j], start=(n == 0), stop=(n == PARTS - 1))
                    ins.then_inc(scattered, 1)

                with pe.Fori(0, HALF // RING) as i:
                    for s in range(RING):
                        up_tile(0, i, s)
                pe.wait_ge(pick_done, layer + 1)
                pe.wait_ge(score_out, 8 * (layer + 1))
                for dst, src in ((gp[:, 0, 0:T], EX[:, 0:T]), (gp[:, 0, T:2 * T], EX[:, T:2 * T]),
                                 (gp[:, 1, 0:T], GT)):
                    for tc in range(TC):
                        ins = nc.tensor.matmul(dst[:, tc * P:(tc + 1) * P], src[:, tc * P:(tc + 1) * P], eye,
                                               start=True, stop=True)
                ins.then_inc(turned, 1)
                moved[0] += 1
                with pe.Fori(0, HALF // RING - 1) as i:
                    for s in range(RING):
                        up_tile(HALF, i, s)
                        if s in (1, 2):
                            scatter(0, i, s - 1)
                for s in range(RING):
                    up_tile(HALF, HALF // RING - 1, s)
                    if s % 2 == 0:
                        scatter(0, HALF // RING - 1, s // 2)

                if layer == 1:
                    pe.wait_ge(x_ready, DC)
                for b in range(4):
                    for q in range(4):
                        nc.tensor.matmul(acc[:, b, q * P:(q + 1) * P], zeros[:], zeros[:], start=(q == 0),
                                         stop=False, skip_group_check=True)
                n0 = AT[layer, "down"]
                for half in range(2):
                    def down_tile(i, s, closing):
                        pe.wait_ge(low_ready, i * RING + (n0 + half * HALF + s + 1))
                        pe.wait_ge(wl_ready, i * RING + (layer * KEYS + half * HALF + s + 1))
                        for c in range(DC):
                            ins = three(acc[:, c // 2, (c % 2) * T:(c % 2 + 1) * T], s, c, s, False, closing, True)
                            if closing and c % 2 and c < DC - 1:
                                ins.then_inc(acc_done, 1)
                        ins.then_inc(product, 1)

                    if half == 0:
                        with pe.Fori(0, HALF // RING - 1) as i:
                            for s in range(RING):
                                down_tile(i, s, False)
                                if s in (1, 2):
                                    scatter(1, i, s - 1)
                        for s in range(RING):
                            down_tile(HALF // RING - 1, s, False)
                            if s % 2 == 0:
                                scatter(1, HALF // RING - 1, s // 2)
                    else:
                        with pe.Fori(0, HALF // RING - 1) as i:
                            for s in range(RING):
                                down_tile(i, s, False)
                        for s in range(RING):
                            if layer == 0 and s == RING - 1:
                                pe.wait_ge(next_used, NEXT + NEXT * DC)
                                pe.wait_ge(weighted, 2 * SETS)
                                sum_mod((0, 1))
                            down_tile(HALF // RING - 1, s, s == RING - 1)
            square_sums(4)
            spread(4)


def kernel(**inputs):
    import numpy as np
    import concourse.bacc as bacc
    from concourse.bass_utils import run_bass_kernel_spmd

    a = {k: np.asarray(v) for k, v in inputs.items()}

    def chunks(v):
        v = v.reshape(-1, DC, P)
        return v.transpose(2, 0, 1).reshape(P, -1)

    def tiles(w):
        k, n = w.shape
        return w.reshape(k // P, P, n // P, P).transpose(2, 1, 0, 3).reshape(n // P, P, k)

    groups = len(WINDOWS)
    pool_in = tiles(a["pool_w_in"][0]).reshape(groups, -1, P, D)[::-1].reshape(DC, P, D)
    pool_scale = a["pool_scale"].reshape(groups, -1)[::-1].reshape(1, D)
    pool_out = a["pool_w_out"][0].reshape(groups, -1, D)[::-1].reshape(D, D)
    counts = np.array([[1.0 / min(t + 1, w) for t in range(PAD)] for w in WINDOWS], np.float32).reshape(1, -1)
    small = np.concatenate([
        chunks(a["c"]), chunks(a["norm1_g"]), chunks(a["norm2_g"]), chunks(a["b_mod"]), chunks(a["conv_w"]),
        chunks(pool_scale), chunks(a["final_g"]),
        np.broadcast_to(np.arange(P, dtype=np.float32), (P, P)), np.eye(P, dtype=np.float32),
        np.broadcast_to(counts, (P, counts.size))], axis=1)
    order = [g * DC + j for j in range(DC) for g in (1, 2, 0)]
    grp = a["pool_w_grp"][0][::-1].reshape(4, 2, P, 2, P).transpose(0, 2, 3, 1, 4).reshape(4, P, 4 * P)
    arrays = {
        "small": small,
        "x_t": a["x"][0].T.reshape(DC, P, T).transpose(1, 0, 2).reshape(P, DC * T),
        "k_t": np.stack([a["peer_k1"].transpose(0, 2, 1), a["peer_k2"].transpose(0, 2, 1)], axis=2),
        "w_mod": a["w_mod"],
        "conv_in": tiles(a["conv_w_in"][0])[order],
        "conv_out": tiles(a["conv_w_out"][0]),
        "query": np.stack([tiles(w) for w in a["peer_w_q"]]),
        "up": a["peer_u"].reshape(LAYERS, KEYS, P, DC, P).transpose(0, 1, 4, 3, 2).reshape(LAYERS, KEYS, P, D),
        "down": a["peer_v"].reshape(LAYERS, KEYS, P, D),
        "pool_in": pool_in,
        "pool_group": np.concatenate([grp, np.zeros_like(grp)], axis=2),
        "pool_out": tiles(pool_out),
    }
    nc = bacc.Bacc("TRN2", target_bir_lowering=False, num_devices=1)
    args = []
    for name, v in arrays.items():
        arrays[name] = v = np.ascontiguousarray(v)
        args.append(nc.dram_tensor(name, v.shape, mybir.dt.from_np(v.dtype), kind="ExternalInput").ap())
    x_spill = nc.dram_tensor("x_spill", (P, DC * T), F32, kind="Internal").ap()
    out = nc.dram_tensor("out", (P, DC * T), F32, kind="ExternalOutput").ap()
    program(nc, *args, x_spill, out)
    r = run_bass_kernel_spmd(nc, [arrays], core_ids=[0])
    got = np.asarray(r.results[0]["out"])
    return got.reshape(P, DC, T).transpose(2, 1, 0).reshape(1, T, D)
```
